# Optimizing a Trainium2 kernel written in Bass

```python
import math
import jax, jax.numpy as jnp
from jax import lax
import numpy as np

D_MODEL = 2048
BATCH = 1
SEQ = 256
DEPTH = 1

CHUNK = 64
EPS = 1e-6
ATT_HEADS = 32
ATT_KV_HEADS = 8
HEAD_DIM = 64
ATT_GROUP = ATT_HEADS // ATT_KV_HEADS
ATT_Q = ATT_HEADS * HEAD_DIM
ATT_KV = ATT_KV_HEADS * HEAD_DIM
WINDOW = 128
WINDOW_CHUNKS = WINDOW // CHUNK
ROPE_THETA = 10000.0
SSD_HEADS = 32
SSD_HEAD_DIM = 64
SSD_INNER = SSD_HEADS * SSD_HEAD_DIM
SSD_GROUPS = 4
SSD_HPG = SSD_HEADS // SSD_GROUPS
SSD_STATE = 128
CONV_WIDTH = 4
CONV_CH = SSD_INNER + 2 * SSD_GROUPS * SSD_STATE
N_IN = ATT_Q + 2 * ATT_KV + SSD_INNER + CONV_CH + SSD_HEADS + 2 * D_MODEL
MEM_LEN = 256
XA_HEADS = 4
XA_HEAD_DIM = 128
XA_WIDTH = XA_HEADS * XA_HEAD_DIM
FFN_HIDDEN = -(-8 * D_MODEL // (3 * 256)) * 256

kernel_name = "hybrid_swa_sink_ssd_gated_merge_encoder"

def _rmsnorm(x, g):
    xf = x.astype(jnp.float32)
    y = xf * lax.rsqrt(jnp.mean(xf * xf, axis=-1, keepdims=True) + EPS)
    return (y * g.astype(jnp.float32)).astype(x.dtype)

def _split(t, sizes):
    outs, start = [], 0
    for s in sizes:
        outs.append(t[..., start:start + s])
        start += s
    return outs

def _rope_tables(positions):
    inv_freq = ROPE_THETA ** (-jnp.arange(0, HEAD_DIM, 2, dtype=jnp.float32) / HEAD_DIM)
    ang = positions.astype(jnp.float32)[..., None] * inv_freq
    return jnp.cos(ang)[:, :, None, :], jnp.sin(ang)[:, :, None, :]

def _apply_rope(t, cos, sin):
    tf = t.astype(jnp.float32)
    t1, t2 = tf[..., :HEAD_DIM // 2], tf[..., HEAD_DIM // 2:]
    return jnp.concatenate([t1 * cos - t2 * sin, t2 * cos + t1 * sin], axis=-1).astype(t.dtype)

def _shift_chunks(t, j):
    if j == 0:
        return t
    pad = [(0, 0), (j, 0)] + [(0, 0)] * (t.ndim - 2)
    return jnp.pad(t, pad)[:, :-j]

def _window_sink_attention(q, k, v, sink):
    b, l, _, _ = q.shape
    nc = l // CHUNK
    qb = q.reshape(b, nc, CHUNK, ATT_KV_HEADS, ATT_GROUP, HEAD_DIM)
    kb = k.reshape(b, nc, CHUNK, ATT_KV_HEADS, HEAD_DIM)
    vb = v.reshape(b, nc, CHUNK, ATT_KV_HEADS, HEAD_DIM)
    kw = jnp.concatenate([_shift_chunks(kb, j) for j in range(WINDOW_CHUNKS - 1, -1, -1)], axis=2)
    vw = jnp.concatenate([_shift_chunks(vb, j) for j in range(WINDOW_CHUNKS - 1, -1, -1)], axis=2)
    s = jnp.einsum('bcqkgd,bcskd->bckgqs', qb, kw).astype(jnp.float32) * (HEAD_DIM ** -0.5)
    chunk_idx = jnp.arange(nc)[:, None]
    slot_chunk = jnp.arange(WINDOW_CHUNKS * CHUNK)[None, :] // CHUNK - (WINDOW_CHUNKS - 1)
    valid = (chunk_idx + slot_chunk) >= 0
    s = jnp.where(valid[None, :, None, None, None, :], s, -jnp.inf)
    sk = sink.astype(jnp.float32).reshape(1, 1, ATT_KV_HEADS, ATT_GROUP, 1, 1)
    m = jnp.maximum(jnp.max(s, axis=-1, keepdims=True), sk)
    p = jnp.exp(s - m)
    p = p / (jnp.sum(p, axis=-1, keepdims=True) + jnp.exp(sk - m))
    o = jnp.einsum('bckgqs,bcskd->bcqkgd', p.astype(v.dtype), vw)
    return o.reshape(b, l, ATT_Q)

def _causal_depthwise_conv(u, w, bias):
    out = lax.conv_general_dilated(
        u, w[:, None, :].astype(u.dtype), window_strides=(1,), padding=[(CONV_WIDTH - 1, 0)],
        dimension_numbers=('NWC', 'WIO', 'NWC'), feature_group_count=u.shape[-1])
    return out + bias.astype(u.dtype)

def _ssd_chunked(xs, dt, a, bm, cm):
    b, l = xs.shape[:2]
    nc = l // CHUNK
    x = xs.astype(jnp.float32).reshape(b, nc, CHUNK, SSD_GROUPS, SSD_HPG, SSD_HEAD_DIM)
    dt5 = dt.reshape(b, nc, CHUNK, SSD_GROUPS, SSD_HPG)
    bmf = bm.astype(jnp.float32).reshape(b, nc, CHUNK, SSD_GROUPS, SSD_STATE)
    cmf = cm.astype(jnp.float32).reshape(b, nc, CHUNK, SSD_GROUPS, SSD_STATE)
    da = dt5 * a.reshape(SSD_GROUPS, SSD_HPG)
    cs = jnp.cumsum(da, axis=2)
    xdt = x * dt5[..., None]
    seg = cs[:, :, :, None] - cs[:, :, None, :]
    causal = jnp.tril(jnp.ones((CHUNK, CHUNK), dtype=bool))[:, :, None, None]
    lmat = jnp.exp(jnp.where(causal, seg, -jnp.inf))
    cb = jnp.einsum('bclgn,bcsgn->bclsg', cmf, bmf)
    y_diag = jnp.einsum('bclsg,bclsgr,bcsgrp->bclgrp', cb, lmat, xdt)
    decay_to_end = jnp.exp(cs[:, :, -1:] - cs)
    states = jnp.einsum('bclgn,bclgr,bclgrp->bcgrpn', bmf, decay_to_end, xdt)
    chunk_decay = jnp.exp(cs[:, :, -1])

    def step(h, inp):
        st, dec = inp
        return h * dec[..., None, None] + st, h

    h0 = jnp.zeros((b, SSD_GROUPS, SSD_HPG, SSD_HEAD_DIM, SSD_STATE), jnp.float32)
    _, prev = lax.scan(step, h0, (jnp.moveaxis(states, 1, 0), jnp.moveaxis(chunk_decay, 1, 0)))
    prev = jnp.moveaxis(prev, 0, 1)
    y_off = jnp.einsum('bclgn,bcgrpn,bclgr->bclgrp', cmf, prev, jnp.exp(cs))
    return (y_diag + y_off).reshape(b, l, SSD_HEADS, SSD_HEAD_DIM)

def _gated_group_rmsnorm(y, z, g):
    yz = (y.astype(jnp.float32) * jax.nn.silu(z.astype(jnp.float32)))
    sh = yz.shape
    yg = yz.reshape(sh[:-1] + (SSD_GROUPS, SSD_INNER // SSD_GROUPS))
    yg = yg * lax.rsqrt(jnp.mean(yg * yg, axis=-1, keepdims=True) + EPS)
    return (yg.reshape(sh) * g.astype(jnp.float32)).astype(y.dtype)

def _hybrid_mixer(h, cos, sin, w_in, conv_w, conv_b, dt_bias, a_log, d_skip, ssd_norm_g,
                  attn_sink, w_attn_branch, w_ssd_branch, w_out):
    b, l, _ = h.shape
    proj = h @ w_in
    q, k, v, z, xbc, dt_raw, g_att, g_ssd = _split(
        proj, [ATT_Q, ATT_KV, ATT_KV, SSD_INNER, CONV_CH, SSD_HEADS, D_MODEL, D_MODEL])
    q = _apply_rope(q.reshape(b, l, ATT_HEADS, HEAD_DIM), cos, sin)
    k = _apply_rope(k.reshape(b, l, ATT_KV_HEADS, HEAD_DIM), cos, sin)
    v = v.reshape(b, l, ATT_KV_HEADS, HEAD_DIM)
    att = _window_sink_attention(q, k, v, attn_sink)
    xbc = jax.nn.silu(_causal_depthwise_conv(xbc, conv_w, conv_b))
    xs, bm, cm = _split(xbc, [SSD_INNER, SSD_GROUPS * SSD_STATE, SSD_GROUPS * SSD_STATE])
    xs = xs.reshape(b, l, SSD_HEADS, SSD_HEAD_DIM)
    bm = bm.reshape(b, l, SSD_GROUPS, SSD_STATE)
    cm = cm.reshape(b, l, SSD_GROUPS, SSD_STATE)
    dt = jax.nn.softplus(dt_raw.astype(jnp.float32) + dt_bias.astype(jnp.float32))
    a = -jnp.exp(a_log.astype(jnp.float32))
    y = _ssd_chunked(xs, dt, a, bm, cm) + d_skip.astype(jnp.float32)[:, None] * xs.astype(jnp.float32)
    y = _gated_group_rmsnorm(y.reshape(b, l, SSD_INNER).astype(h.dtype), z, ssd_norm_g)
    merged = jax.nn.sigmoid(g_att) * (att @ w_attn_branch) + jax.nn.sigmoid(g_ssd) * (y @ w_ssd_branch)
    return merged @ w_out

def _memory_cross_attention(h, mem_n, wq, wk, wv, wo):
    b, l, _ = h.shape
    q = (h @ wq).reshape(b, l, XA_HEADS, XA_HEAD_DIM)
    k = (mem_n @ wk).reshape(b, MEM_LEN, XA_HEADS, XA_HEAD_DIM)
    v = (mem_n @ wv).reshape(b, MEM_LEN, XA_HEADS, XA_HEAD_DIM)
    s = jnp.einsum('blhd,bmhd->bhlm', q, k).astype(jnp.float32) * (XA_HEAD_DIM ** -0.5)
    p = jax.nn.softmax(s, axis=-1).astype(v.dtype)
    o = jnp.einsum('bhlm,bmhd->blhd', p, v).reshape(b, l, XA_WIDTH)
    return o @ wo

def _swiglu(h, wg, wu, wd):
    return (jax.nn.silu(h @ wg) * (h @ wu)) @ wd

def setup_inputs(seed: int = 0) -> dict:
    key = jax.random.key(seed)
    ks = iter(jax.random.split(key, 40))
    f32 = jnp.float32

    def nrm(shape, fan_in):
        return jax.random.normal(next(ks), shape, f32) * (fan_in ** -0.5)

    def gain(shape):
        return 1.0 + 0.05 * jax.random.normal(next(ks), shape, f32)

    x = jax.random.normal(next(ks), (BATCH, SEQ, D_MODEL), f32)
    mem = jax.random.normal(next(ks), (BATCH, MEM_LEN, D_MODEL), f32)
    offsets = jax.random.randint(next(ks), (BATCH, 1), 0, 64) * CHUNK
    positions = (offsets + jnp.arange(SEQ, dtype=jnp.int32)[None, :]).astype(jnp.int32)

    u = jax.random.uniform(next(ks), (DEPTH, SSD_HEADS), f32)
    dt0 = jnp.exp(u * (math.log(0.1) - math.log(1e-3)) + math.log(1e-3))
    dt_bias = dt0 + jnp.log(-jnp.expm1(-dt0))
    a_log = jnp.log(jax.random.uniform(next(ks), (DEPTH, SSD_HEADS), f32, 1.0, 16.0))

    return {
        "x": x,
        "mem": mem,
        "positions": positions,
        "mix_pre_g": gain((DEPTH, D_MODEL)),
        "mix_post_g": gain((DEPTH, D_MODEL)),
        "w_in": nrm((DEPTH, D_MODEL, N_IN), D_MODEL),
        "conv_w": nrm((DEPTH, CONV_WIDTH, CONV_CH), CONV_WIDTH),
        "conv_b": 0.02 * jax.random.normal(next(ks), (DEPTH, CONV_CH), f32),
        "dt_bias": dt_bias,
        "a_log": a_log,
        "d_skip": 1.0 + 0.1 * jax.random.normal(next(ks), (DEPTH, SSD_HEADS), f32),
        "ssd_norm_g": gain((DEPTH, SSD_INNER)),
        "attn_sink": 0.5 * jax.random.normal(next(ks), (DEPTH, ATT_HEADS), f32),
        "w_attn_branch": nrm((DEPTH, ATT_Q, D_MODEL), ATT_Q),
        "w_ssd_branch": nrm((DEPTH, SSD_INNER, D_MODEL), SSD_INNER),
        "w_out": nrm((DEPTH, D_MODEL, D_MODEL), D_MODEL),
        "xa_pre_g": gain((DEPTH, D_MODEL)),
        "xa_mem_g": gain((DEPTH, D_MODEL)),
        "xa_post_g": gain((DEPTH, D_MODEL)),
        "xa_wq": nrm((DEPTH, D_MODEL, XA_WIDTH), D_MODEL),
        "xa_wk": nrm((DEPTH, D_MODEL, XA_WIDTH), D_MODEL),
        "xa_wv": nrm((DEPTH, D_MODEL, XA_WIDTH), D_MODEL),
        "xa_wo": nrm((DEPTH, XA_WIDTH, D_MODEL), XA_WIDTH),
        "ffn_pre_g": gain((DEPTH, D_MODEL)),
        "ffn_post_g": gain((DEPTH, D_MODEL)),
        "ffn_wg": nrm((DEPTH, D_MODEL, FFN_HIDDEN), D_MODEL),
        "ffn_wu": nrm((DEPTH, D_MODEL, FFN_HIDDEN), D_MODEL),
        "ffn_wd": nrm((DEPTH, FFN_HIDDEN, D_MODEL), FFN_HIDDEN),
    }

def reference(x, mem, positions, mix_pre_g, mix_post_g, w_in, conv_w, conv_b, dt_bias, a_log, d_skip,
              ssd_norm_g, attn_sink, w_attn_branch, w_ssd_branch, w_out, xa_pre_g, xa_mem_g, xa_post_g,
              xa_wq, xa_wk, xa_wv, xa_wo, ffn_pre_g, ffn_post_g, ffn_wg, ffn_wu, ffn_wd):
    cos, sin = _rope_tables(positions)
    for i in range(DEPTH):
        h = _rmsnorm(x, mix_pre_g[i])
        mix = _hybrid_mixer(h, cos, sin, w_in[i], conv_w[i], conv_b[i], dt_bias[i], a_log[i], d_skip[i],
                            ssd_norm_g[i], attn_sink[i], w_attn_branch[i], w_ssd_branch[i], w_out[i])
        x = x + _rmsnorm(mix, mix_post_g[i])
        h = _rmsnorm(x, xa_pre_g[i])
        mem_n = _rmsnorm(mem, xa_mem_g[i])
        xa = _memory_cross_attention(h, mem_n, xa_wq[i], xa_wk[i], xa_wv[i], xa_wo[i])
        x = x + _rmsnorm(xa, xa_post_g[i])
        h = _rmsnorm(x, ffn_pre_g[i])
        x = x + _rmsnorm(_swiglu(h, ffn_wg[i], ffn_wu[i], ffn_wd[i]), ffn_post_g[i])
    return x


_drawn_inputs = setup_inputs


def setup_inputs(seed=0):
    import zlib

    import numpy as np

    out = dict(_drawn_inputs(seed))
    spreads = {}
    factors = {'attn_sink': 8.0}
    for name, (base, spread) in spreads.items():
        noise = np.random.default_rng([zlib.crc32(name.encode()), seed]).standard_normal(out[name].shape)
        drawn = base * np.exp(spread * noise) if base else spread * noise
        out[name] = __import__('jax').numpy.asarray(drawn.astype(out[name].dtype))
    for name, factor in factors.items():
        out[name] = (out[name] * factor).astype(out[name].dtype)
    return out
```

```python
from contextlib import ExitStack

import numpy as np

import concourse.bass as bass
from concourse import mybir

F32 = mybir.dt.float32
FR = mybir.dt.float32r
BF16 = mybir.dt.bfloat16
I32 = mybir.dt.int32
ACT = mybir.ActivationFunctionType
ALU = mybir.AluOpType
AX = mybir.AxisListType

P = 128
SEQ = 256
M = SEQ // P
D = 2048
KT = D // P
COLS = 512
EPS = 1e-6
HD = 64
HEADS = 32
KV = 8
GROUPS = 4
HPG = HEADS // GROUPS
ATT_SCALE = HD ** -0.5
XH = 4
X_SCALE = P ** -0.5
FFN = 5632
FBLOCKS = FFN // COLS
FKT = FFN // P
NEG = -1e30

Q0, K0, V0, Z0 = 0, 2048, 2560, 3072
XS0, B0, C0, DT0, GA0, GS0 = 5120, 7168, 7680, 8192, 8224, 10272

RAW = 8
SPLIT = 4
AHEAD = 4
KPC = 2
CPB = KT // KPC

MIX_ORDER = [("k", 0), ("v", 0), ("q", 0), ("B", 0), ("q", 1), ("C", 0), ("dt", 0), ("q", 2), ("xs", 0),
             ("q", 3), ("z", 0), ("xs", 1), ("z", 1), ("xs", 2), ("z", 2), ("xs", 3), ("z", 3)]
for _j in range(4):
    MIX_ORDER += [("ga", _j), ("att", _j)]
MIX_ORDER += [("gs", 0), ("y", 0)]
START, ACC = {}, {}
_n = _blk = 0
for _b in MIX_ORDER:
    START[_b] = _n
    if _b[0] == "dt":
        _n += 1
        continue
    ACC[_b] = _blk
    _n += CPB
    _blk += 1
N_LOOP_Y, BLK_LOOP_Y = _n, _blk
LOOP_Y = 3
N_OUT, BLK_OUT = _n + LOOP_Y * 2 * CPB, _blk + LOOP_Y * 2
N_XK, BLK_XK = N_OUT + 4 * CPB, BLK_OUT + 4
N_XQ, BLK_XQ = N_XK + CPB, BLK_XK + 1
N_XV, BLK_XV = N_XQ + CPB, BLK_XQ + 1
N_XO, BLK_XO = N_XV + CPB, BLK_XV + 1
N_FFN, BLK_FFN = N_XO + 8, BLK_XO + 4
N_DOWN, BLK_DOWN = N_FFN + FBLOCKS * 2 * CPB, BLK_FFN + 2 * FBLOCKS
DOWN_UNROLL = 4
DOWN_TURNS = FKT // DOWN_UNROLL
N_END = N_DOWN + 2 * FKT


def end_of(b):
    return START[b] + CPB


PE_STEPS, ACT_STEPS, DVE_STEPS = {}, {}, {}


def at(n, arg, pe=(), act=(), dve=()):
    for table, steps in ((PE_STEPS, pe), (ACT_STEPS, act), (DVE_STEPS, dve)):
        for name, behind in steps:
            table.setdefault(n + behind, []).append((name, arg))


at(0, 0, act=[("squares_x", 4), ("root_x", 6), ("angles", 6)], dve=[("angles", 4), ("norm_x", 7)])
at(end_of(("k", 0)), 0, pe=[("turn_k", 5)], act=[("keep_k", 9)], dve=[("rope_k", 3)])
at(end_of(("v", 0)), 0, act=[("keep_v", 3)])
for _b in range(4):
    _n = end_of(("q", _b))
    at(_n, _b, pe=[("turn_q", 3)], act=[("keep_q", 7)], dve=[("rope_q", 3)])
    for _h in range(2):
        at(_n + 5 * _h, 2 * _b + _h,
           pe=[("scores", 6), ("turn_p", 10), ("pv", 12)],
           act=[("exponents", 11), ("keep_p", 14), ("keep_o", 16)],
           dve=[("maxima", 10), ("probabilities", 12), ("keep_p", 14), ("keep_o", 16)])
at(START[("dt", 0)], 0, pe=[("turn_dt", 2), ("decay_sums", 8)],
   act=[("keep_dt", 4), ("delta_exp", 7), ("keep_sums", 12), ("sums_hi", 14)],
   dve=[("delta_in", 6), ("delta_series", 8), ("delta_out", 9), ("keep_sums", 13), ("sums_lo", 15)])
for _i, _b in enumerate([("B", 0), ("C", 0)] + [("xs", g) for g in range(4)]):
    _n = end_of(_b)
    at(_n, _i, pe=[("turn_u", 2)], act=[("keep_u", 3), ("last_tap", 6), ("silu", 7)], dve=[("taps", 6)])
    if _b[0] == "xs":
        at(_n, _b[1], pe=[("turn_xs", 7)], act=[("keep_xs", 11)], dve=[("keep_xs", 11)])
for _g in range(GROUPS):
    _n = end_of(("z", _g))
    at(_n, _g, pe=[("cb", 1)], act=[("keep_z", 3), ("keep_cb", 5)])
    at(_n, 3 * _g, pe=[("seg", 1), ("y_part", 4)], act=[("decay", 5)], dve=[("decay", 6)])
    at(_n, 3 * _g + 1, pe=[("seg", 4)], act=[("decay", 8)], dve=[("decay", 9)])
    at(_n, 2 * _g, act=[("gate_root", 10)], dve=[("gate_y", 9), ("norm_y", 11)])
    _n += 0 if _g else 4
    at(_n, 3 * _g + 1, pe=[("y_part", 7)])
    at(_n, 3 * _g + 2, pe=[("seg", 7), ("y_part", 10)], act=[("decay", 11)], dve=[("decay", 12)])
    at(_n, 2 * _g + 1, act=[("gate_root", 14)], dve=[("gate_y", 14), ("norm_y", 15)])
    at(_n, _g, pe=[("turn_y", 13)], act=[("keep_y", 17)], dve=[("keep_y", 17)])
for _j in range(4):
    at(end_of(("ga", _j)), ("ga", _j), act=[("sigmoid", 3)])
    at(end_of(("att", _j)), _j, dve=[("merge_att", 3)])
at(end_of(("gs", 0)), ("gs", 0), act=[("sigmoid", 3)])
for _table in (PE_STEPS, ACT_STEPS, DVE_STEPS):
    assert max(_table) < N_LOOP_Y

BANKS = {"turn_k": (0, 1, 2, 3), "turn_q": (2, 3), "scores": (0, 1, 2), "turn_p": (0, 1, 2), "pv": (3, 0),
         "turn_dt": (), "decay_sums": (2,), "turn_u": (0, 1), "turn_xs": (0, 1), "cb": (2,), "seg": (0, 1),
         "turn_y": (2, 3)}
TURN = {}
_used = [0] * 4


def use_banks(key, banks):
    for b in banks:
        TURN[key, b] = _used[b]
        _used[b] += 1


X_T = 8
for _j in range(X_T):
    use_banks(("x", _j), (_j % 4,))
for _n in range(N_LOOP_Y):
    if _n == START[("dt", 0)]:
        use_banks(("dt", 0), (3,))
    for _name, _arg in PE_STEPS.get(_n, []):
        if _name == "y_part":
            if _arg % 3 != 2:
                use_banks(("y_bank", 2 * (_arg // 3) + _arg % 3), (3,))
        else:
            use_banks((_name, _arg), BANKS[_name])
for _i in range(LOOP_Y + 1):
    use_banks(("merged", _i), (0, 1))
for _j in range(X_T):
    use_banks(("mem", _j), (_j % 4,))
for _j in range(X_T):
    use_banks(("h2", _j), (_j % 4,))
use_banks(("xk", 0), (0, 1))
use_banks(("xq", 0), (2, 3))
use_banks(("xscores", 0), (0, 1, 2, 3))
use_banks(("xturn_p0", 0), (0, 1))
use_banks(("xturn_p1", 0), (2, 3))
use_banks(("xpv", 0), (0, 1))
for _j in range(X_T):
    use_banks(("h3", _j), (_j % 4,))
for _i in range(FBLOCKS):
    use_banks(("hidden", _i), (0, 1))
use_banks(("down", 0), (0, 1, 2, 3))

CONV_UNITS = [("B", 0), ("C", 0)] + [("xs", g) for g in range(GROUPS)]

G_MIX, G_XA, G_MEM, G_FFN, G_SSD, CONV_B, CONV_W = 0, 16, 32, 48, 64, 80, 104
PARAMS = CONV_W + 96
R_DTB, R_ALOG, R_DSKIP, R_SINK = 0, 32, 64, 96
ROWS = 128
C_IDENT, C_TRI, C_AM0, C_AM1, C_CNEG, C_FREQ, C_SEL, C_EPS, C_TOTAL = 0, 128, 256, 384, 576, 704, 736, 768, 769


def trunk(nc, x, mem, positions, w_in, w_attn_branch, w_ssd_branch, w_out, xa_wq, xa_wk, xa_wv, xa_wo,
          ffn_wg, ffn_wu, ffn_wd, params, rows, post_gains, consts, out):
    ctx = ExitStack()
    with ctx:
        def sem(name):
            return ctx.enter_context(nc.semaphore(name))

        base = 17408
        place = [base]

        def sb(name, shape, dt=F32, offset=None):
            size = int(np.prod(shape[1:])) * (2 if dt == BF16 else 4)
            t = nc.alloc_sbuf_tensor_at(name, shape, dt, offset=place[0] if offset is None else offset)
            if offset is None:
                place[0] += -(-size // 32) * 32
            return t

        KB = 1024
        raw = sb("raw", [P, RAW, KPC * COLS])
        hi = sb("hi", [P, SPLIT, KPC * COLS], FR)
        lo = sb("lo", [P, SPLIT, KPC * COLS], FR)
        at_a = place[0]
        aT = sb("aT", [P, 2, KT, SEQ], FR)
        at_b = place[0]
        bT = sb("bT", [P, 2, KT, SEQ], FR)
        at_c = place[0]
        cT = sb("cT", [P, 2, KT, SEQ], FR)
        at_w = place[0]
        kT = sb("kT", [P, KV, SEQ], offset=at_c)
        vv = sb("vv", [P, M, KV, 2, HD], offset=at_c + 8 * KB)
        qs = sb("qs", [P, M, COLS], offset=at_c + 16 * KB)
        qT = sb("qT", [P, 4, SEQ], offset=at_c + 20 * KB)
        pT = sb("pT", [P, 3, COLS], offset=at_c + 24 * KB)
        swapped = sb("swapped", [P, COLS], offset=at_c + 30 * KB)
        xm = sb("xm", [P, M, D], offset=at_w)
        mix = sb("mix", [P, M, D], offset=at_w + 16 * KB)
        kk = sb("kk", [P, M, KV, 2, HD], offset=at_w)
        bcT = sb("bcT", [P, 2, 4, SEQ], offset=at_w)
        uc = sb("uc", [P, 4 * SEQ], offset=at_w + 8 * KB)
        xs = sb("xs", [P, M, COLS], offset=at_w + 12 * KB)
        xdt = sb("xdt", [P, M, COLS], offset=at_w + 16 * KB)
        lm = sb("lm", [P, HPG, P], offset=at_w + 20 * KB)
        yy = sb("yy", [P, M, COLS], offset=at_w + 24 * KB)
        sz = sb("sz", [P, M, COLS], offset=at_w + 28 * KB)
        place[0] += 32 * KB
        p0 = sb("p0", [P, 4, P])
        p1 = sb("p1", [P, 4, SEQ])
        gate = sb("gate", [P, M, COLS], offset=place[0] - 4 * KB)
        csq = sb("csq", [2 * HEADS, 3, P], FR)
        cbs = sb("cbs", [P, 3 * P])
        dt = sb("dt", [P, M, HEADS])
        junk = sb("junk", [P, D], offset=at_c)
        at_t = at_w + 20 * KB
        da2 = sb("da2", [P, M, 2, HEADS], offset=at_t)
        csf = sb("csf", [2 * HEADS, 3, P], offset=at_t + 512)
        chi = sb("chi", [2 * HEADS, 3, P], FR, offset=at_t + 2048)
        sp = sb("sp", [P, 6, M * HEADS], offset=at_t + 3584)
        dtT = sb("dtT", [HEADS, SEQ], offset=at_t + 5120)
        ident = sb("ident", [P, P])
        tri = sb("tri", [P, P])
        am0 = sb("am0", [P, P])
        am1 = sb("am1", [P, 192])
        identb = sb("identb", [P, P], BF16)
        cnegb = sb("cnegb", [P, P], BF16)
        sel = sb("sel", [2 * HEADS, 2, HEADS], FR)
        rope = sb("rope", [P, 3, M, 32])
        par = sb("par", [P, PARAMS])
        row = sb("row", [P, ROWS])
        ssq = sb("ssq", [P, 7, M, 4])
        rstd = sb("rstd", [P, 7, M])
        ysq = sb("ysq", [P, M])
        yrs = sb("yrs", [P, M])
        eps = sb("eps", [P, 1])
        mx = sb("mx", [P, 8])
        nmx = sb("nmx", [P, 8])
        esk = sb("esk", [P, 8])
        rsum = sb("rsum", [P, 8])
        assert place[0] <= 229344, place[0]
        ctmp = sb("ctmp", [P, C_TOTAL], offset=at_w + 32 * KB)
        pos = sb("pos", [P, M], I32, offset=at_w + 35 * KB + 64)
        ang = sb("ang", [P, 6, M * 32], offset=at_w + 35 * KB + 128)
        gb = sb("gb", [P, D], offset=at_c + 8 * KB)
        xr = sb("xr", [P, M, D], offset=at_c + 16 * KB)
        gx = sb("gx", [P, D], offset=at_b)
        xqk = sb("xqk", [P, M, COLS], offset=at_b + 8 * KB)
        xqT = sb("xqT", [P, XH, SEQ], offset=at_b + 12 * KB)
        xkT = sb("xkT", [P, XH, SEQ], offset=at_b + 16 * KB)
        xv = sb("xv", [P, M, COLS], offset=at_b + 20 * KB)
        oT = sb("oT", [P, 2, XH, SEQ], FR, offset=at_b + 24 * KB)
        xp = sb("xp", [P, M, XH, SEQ], offset=at_w + 16 * KB)
        xpT = sb("xpT", [P, M, XH, SEQ], offset=at_w + 24 * KB)
        hid = sb("hid", [P, M, COLS], offset=at_w + 16 * KB)
        gf = sb("gf", [P, D], offset=at_w + 20 * KB)
        scaled = sb("scaled", [P, 2, COLS], offset=at_w + 28 * KB)
        squared = sb("squared", [P, 4, COLS], offset=at_b)
        hT = sb("hT", [P, FKT, SEQ], offset=at_b)
        hq = sb("hq", [P, DOWN_UNROLL, 2, SEQ], FR, offset=at_b + 44 * KB)

        acc = ctx.enter_context(nc.psum_tensor("acc", [P, 4, COLS], F32))
        X = ctx.enter_context(nc.psum_tensor("X", [P, 4, COLS], F32))

        raw_loaded = [sem(f"raw_loaded{s}") for s in range(RAW)]
        hi_ready, lo_ready, chunk_used = sem("hi_ready"), sem("lo_ready"), sem("chunk_used")
        acc_free = sem("acc_free")
        bank_full = [sem(f"bank_full{b}") for b in range(4)]
        bank_free = [sem(f"bank_free{b}") for b in range(4)]
        x_in = [sem(f"x_in{h}") for h in range(2)]
        ident_in, consts_in, pos_in, mem_in, x_again, gain_in = (
            sem(s) for s in ("ident_in", "consts_in", "pos_in", "mem_in", "x_again", "gain_in"))
        out_stored, load_turn = sem("out_stored"), sem("load_turn")
        act_step, dve_step = sem("act_step"), sem("dve_step")
        consts_ready = sem("consts_ready")
        angles_ready, rope_ready = sem("angles_ready"), sem("rope_ready")
        sum_ready, root_ready, norm_ready = (sem(s) for s in ("sum_ready", "root_ready", "norm_ready"))
        block_sq = sem("block_sq")
        t_hi = sem("t_hi")
        k_roped, q_roped = sem("k_roped"), sem("q_roped")
        max_ready, exp_ready, probs_ready = (sem(s) for s in ("max_ready", "exp_ready", "probs_ready"))
        even_scores, o_hi = sem("even_scores"), sem("o_hi")
        tap_ready, silu_ready, xs_ready = (sem(s) for s in ("tap_ready", "silu_ready", "xs_ready"))
        sp_in, sp_exp, da_ready = (sem(s) for s in ("sp_in", "sp_exp", "da_ready"))
        dt_kept, cse_ready, chi_ready, csq_lo = (
            sem(s) for s in ("dt_kept", "cse_ready", "chi_ready", "csq_lo"))
        m_ready, y_done = sem("m_ready"), sem("y_done")
        y_gated, y_root, y_normed = (sem(s) for s in ("y_gated", "y_root", "y_normed"))
        yT_hi = sem("yT_hi")
        merged_ready, merged_hi = sem("merged_ready"), sem("merged_hi")
        resid_ready = sem("resid_ready")
        xmax_ready, xp_ready, xo_hi = (sem(s) for s in ("xmax_ready", "xp_ready", "xo_hi"))
        hq_hi, hq_lo = sem("hq_hi"), sem("hq_lo")
        down_done, out_ready = sem("down_done"), sem("out_ready")

        def wait_bank(eng, key, b):
            eng.wait_ge(bank_full[b], TURN[key, b] + 1)

        def take_bank(pe, key, b):
            if TURN[key, b]:
                pe.wait_ge(bank_free[b], TURN[key, b])

        def wait_kept(eng, key, b, more=0):
            eng.wait_ge(bank_free[b], TURN[key, b] + 1 + more)

        def wait_norm(eng, norm):
            eng.wait_ge(norm_ready, {0: 1, 1: 2, 3: 3, 5: 4}[norm])

        def wait_block(eng, blk, more=0):
            eng.wait_ge(acc_free, 2 * (blk + 1) + more)

        block = ctx.enter_context(nc.Block())

        @block.sync
        def _(sp_):
            def load(n, turns, i, dst, src):
                slot, count = n % RAW, n // RAW + 1
                if n >= RAW:
                    sp_.wait_ge(lo_ready, n - RAW + 1 + turns * i)
                if turns:
                    sp_.sem_inc(load_turn, 1)
                sp_.dma_start(dst(raw[:, slot, :]), src).then_inc(raw_loaded[slot], 16)

            def load_block(n, turns, i, w, col, k_tiles=KT):
                rows_ = w.rearrange("(t p) n -> p t n", p=P)
                for c in range(k_tiles // KPC):
                    load(n + c, turns, i, lambda s: s.rearrange("p (k n) -> p k n", k=KPC),
                         rows_[:, c * KPC:(c + 1) * KPC, col])

            for t, c0, sem_ in ((ident, C_IDENT, ident_in), (ctmp, 0, consts_in), (tri, C_TRI, consts_in),
                                (am0, C_AM0, consts_in), (am1, C_AM1, consts_in)):
                sp_.dma_start(t[:], consts[:, c0:c0 + t.shape[1]]).then_inc(sem_, 16)
            sp_.dma_start(par[:], params).then_inc(consts_in, 16)
            sp_.dma_start(row[:], rows.to_broadcast([P, ROWS])).then_inc(consts_in, 16)
            sp_.dma_start(pos[:], positions).then_inc(pos_in, 16)
            columns = {"q": Q0, "k": K0, "v": V0, "z": Z0, "xs": XS0, "B": B0, "C": C0, "ga": GA0, "gs": GS0}
            for b in MIX_ORDER:
                kind, j = b
                if kind == "dt":
                    load(START[b], 0, 0, lambda s: s[:, 0:KT * HEADS].rearrange("p (k n) -> p k n", k=KT),
                         w_in[:, DT0:DT0 + HEADS].rearrange("(t p) n -> p t n", p=P))
                    continue
                w = {"att": w_attn_branch, "y": w_ssd_branch}.get(kind, w_in)
                c0 = columns.get(kind, 0) + j * COLS
                load_block(START[b], 0, 0, w, slice(c0, c0 + COLS))
            with sp_.Fori(0, LOOP_Y) as i:
                load_block(N_LOOP_Y, 2 * CPB, i, w_in, bass.ds((i + 1) * COLS + GS0, COLS))
                load_block(N_LOOP_Y + CPB, 2 * CPB, i, w_ssd_branch, bass.ds((i + 1) * COLS, COLS))
            for j in range(4):
                load_block(N_OUT + j * CPB, 0, 0, w_out, slice(j * COLS, (j + 1) * COLS))
                if j == 0:
                    sp_.wait_ge(merged_ready, LOOP_Y + 1)
                    sp_.dma_start(xm[:], mem.rearrange("b (m p) d -> p (b m) d", p=P)).then_inc(mem_in, 16)
                    sp_.wait_ge(chunk_used, N_OUT)
                    sp_.dma_start(gb[:], post_gains[0:1, :].to_broadcast([P, D])).then_inc(gain_in, 16)
                    sp_.dma_start(xr[:], x.rearrange("b (m p) d -> p (b m) d", p=P)).then_inc(x_again, 16)
            load_block(N_XK, 0, 0, xa_wk, slice(0, COLS))
            sp_.wait_ge(chunk_used, N_XK)
            sp_.dma_start(gx[:], post_gains[1:2, :].to_broadcast([P, D])).then_inc(gain_in, 16)
            load_block(N_XQ, 0, 0, xa_wq, slice(0, COLS))
            load_block(N_XV, 0, 0, xa_wv, slice(0, COLS))
            for j in range(4):
                load_block(N_XO + 2 * j, 0, 0, xa_wo, slice(j * COLS, (j + 1) * COLS), k_tiles=XH)
            with sp_.Fori(0, FBLOCKS) as i:
                load_block(N_FFN, 2 * CPB, i, ffn_wg, bass.ds(i * COLS, COLS))
                load_block(N_FFN + CPB, 2 * CPB, i, ffn_wu, bass.ds(i * COLS, COLS))
            sp_.wait_ge(root_ready, 6)
            sp_.dma_start(gf[:], post_gains[2:3, :].to_broadcast([P, D])).then_inc(gain_in, 16)
            for c in range(2 * DOWN_UNROLL):
                k, half = c % DOWN_UNROLL, c // DOWN_UNROLL
                load(N_DOWN + c, 0, 0, lambda s: s, ffn_wd[k * P:(k + 1) * P, half * 1024:(half + 1) * 1024])
            with sp_.Fori(1, DOWN_TURNS) as i:
                for c in range(2 * DOWN_UNROLL):
                    half = c % 2
                    load(N_DOWN + c, 2 * DOWN_UNROLL, i, lambda s: s,
                         ffn_wd[bass.ds((i * DOWN_UNROLL + c // 2) * P, P), half * 1024:(half + 1) * 1024])
            for q in range(2 * M):
                m, cols = q // 2, slice(q % 2 * 2 * COLS, (q % 2 + 1) * 2 * COLS)
                sp_.wait_ge(out_ready, q + 1)
                sp_.dma_start(out[0, m * P:(m + 1) * P, cols], xm[:, m, cols]).then_inc(out_stored, 16)
            sp_.wait_ge(out_stored, 16 * 2 * M)

        @block.tensor
        def _(pe):
            def step(name, arg):
                PE[name](arg)

            def block_products(n, blk, lhs, turns=0, blk_turns=0, i=0, k_tiles=KT, steps=True, ready=None,
                               between=None):
                if blk >= 2:
                    pe.wait_ge(acc_free, 2 * (blk - 1) + 2 * blk_turns * i)
                for c in range(k_tiles // KPC):
                    if ready:
                        ready(c)
                    pe.wait_ge(lo_ready, n + c + 1 + turns * i)
                    s = (n + c) % SPLIT
                    for k in range(KPC):
                        kt = c * KPC + k
                        for m in range(M):
                            o = acc[:, 2 * (blk % 2) + m, :]
                            for a, w in ((0, hi), (1, hi), (0, lo)):
                                last = pe.matmul(o, lhs[:, a, kt, m * P:(m + 1) * P],
                                                 w[:, s, k * COLS:(k + 1) * COLS],
                                                 start=(kt == 0 and a == 0 and w is hi),
                                                 stop=(kt == k_tiles - 1 and w is lo))
                    last.then_inc(chunk_used, 1)
                    if steps:
                        for name, arg in PE_STEPS.get(n + c, []):
                            step(name, arg)
                    if between:
                        between(c)

            def transposed(key, b, parts):
                take_bank(pe, key, b)
                for e, piece in enumerate(parts):
                    last = pe.transpose(X[:, b, e * P:(e + 1) * P], piece, ident[:])
                last.then_inc(bank_full[b], 1)

            def rows_transposed(name, src, turns=range(X_T)):
                for j in turns:
                    transposed((name, j), j % 4, [src[:, m, (2 * j + k) * P:(2 * j + k + 1) * P]
                                                  for k in range(2) for m in range(M)])

            def turn_k(_):
                pe.wait_ge(k_roped, 1)
                for b in range(4):
                    transposed(("turn_k", 0), b, [kk[:, m, 2 * b + g, :, :].rearrange("p e d -> p (e d)")
                                                  for g in range(2) for m in range(M)])

            def turn_q(b):
                pe.wait_ge(q_roped, b + 1)
                for e in range(2):
                    transposed(("turn_q", b), 2 + e, [qs[:, m, (2 * e + t) * P:(2 * e + t + 1) * P]
                                                      for t in range(2) for m in range(M)])

            def scores(u):
                for b in (2, 3):
                    wait_kept(pe, ("turn_q", u // 2), b)
                for b in range(4):
                    wait_kept(pe, ("turn_k", 0), b)
                for b in range(3):
                    take_bank(pe, ("scores", u), b)
                for odd in range(2):
                    r = slice(HD * odd, HD * odd + HD)
                    if odd:
                        pe.wait_ge(even_scores, u + 1)
                    for h in (odd, odd + 2):
                        last = pe.matmul(X[:, 0, h * P:(h + 1) * P], qT[r, 2 * (u % 2) + h // 2, 0:P], kT[r, u, 0:P],
                                         start=True, stop=True)
                    if odd:
                        last.then_inc(bank_full[0], 1)
                    for h in (odd, odd + 2):
                        last = pe.matmul(X[:, 1 + h // 2, odd * SEQ + 64:(odd + 1) * SEQ],
                                         qT[r, 2 * (u % 2) + h // 2, P:SEQ], kT[r, u, 64:SEQ], start=True, stop=True)
                        if odd:
                            last.then_inc(bank_full[1 + h // 2], 1)
                    if not odd:
                        last.then_inc(even_scores, 1)

            def turn_p(u):
                pe.wait_ge(probs_ready, u + 1)
                transposed(("turn_p", u), 0, [p0[:, h, :] for h in range(4)])
                transposed(("turn_p", u), 1, [p1[:, h, 0:P] for h in range(4)])
                transposed(("turn_p", u), 2, [p1[:, h, P:SEQ] for h in range(4)])

            def pv(u):
                for b in range(3):
                    wait_kept(pe, ("turn_p", u), b)
                wait_block(pe, ACC[("v", 0)])
                v = [vv[:, t, u, :, :].rearrange("p e d -> p (e d)") for t in range(M)]
                take_bank(pe, ("pv", u), 3)
                pe.matmul(X[:, 3, :], v[0], pT[:, 0, :], start=True, stop=True).then_inc(bank_full[3], 1)
                take_bank(pe, ("pv", u), 0)
                pe.matmul(X[:, 0, :], v[0], pT[:, 1, :], start=True, stop=False)
                pe.matmul(X[:, 0, :], v[1], pT[:, 2, :], start=False, stop=True).then_inc(bank_full[0], 1)

            def dt_products():
                n = START[("dt", 0)]
                pe.wait_ge(lo_ready, n + 1)
                take_bank(pe, ("dt", 0), 3)
                s = n % SPLIT
                for kt in range(KT):
                    for a, w in ((0, hi), (1, hi), (0, lo)):
                        last = pe.matmul(X[0:HEADS, 3, 0:SEQ], w[:, s, kt * HEADS:(kt + 1) * HEADS], aT[:, a, kt, :],
                                         start=(kt == 0 and a == 0 and w is hi), stop=(kt == KT - 1 and w is lo))
                last.then_inc(chunk_used, 1)

            def turn_dt(_):
                pe.wait_ge(dt_kept, 1)
                for m in range(M):
                    last = pe.transpose(X[:, 3, m * HEADS:(m + 1) * HEADS], dtT[:, m * P:(m + 1) * P],
                                        ident[0:HEADS, 0:HEADS])
                last.then_inc(bank_full[3], 1)

            def decay_sums(_):
                pe.wait_ge(da_ready, 1)
                take_bank(pe, ("decay_sums", 0), 2)
                for m in range(M):
                    last = pe.matmul(X[0:2 * HEADS, 2, m * P:(m + 1) * P],
                                     da2[:, m, :, :].rearrange("p e h -> p (e h)"), tri[:], start=True, stop=True)
                last.then_inc(bank_full[2], 1)

            def turn_u(i):
                wait_block(pe, ACC[CONV_UNITS[i]])
                u3 = uc[:].rearrange("p (m n) -> p m n", m=M)
                for e in range(2):
                    transposed(("turn_u", i), e, [u3[:, m, (2 * e + t) * P:(2 * e + t + 1) * P]
                                                  for t in range(2) for m in range(M)])

            def turn_xs(g):
                pe.wait_ge(silu_ready, 3 + g)
                for m in range(M):
                    transposed(("turn_xs", g), m, [uc[:, c * SEQ + m * P:c * SEQ + (m + 1) * P] for c in range(4)])

            def cb(g):
                pe.wait_ge(silu_ready, 2)
                take_bank(pe, ("cb", g), 2)
                pe.matmul(X[:, 2, 0:SEQ], bcT[:, 0, g, 0:P], bcT[:, 1, g, :], start=True, stop=True)
                pe.matmul(X[:, 2, SEQ:SEQ + P], bcT[:, 0, g, P:SEQ], bcT[:, 1, g, P:SEQ], start=True,
                          stop=True).then_inc(bank_full[2], 1)

            def add_nothing(b, start):
                return pe.matmul(X[:, b, :].rearrange("p (h l) -> p h l", h=4), identb[0:1, :],
                                 cnegb[0:1, :].unsqueeze(1).to_broadcast([1, 4, P]), start=start, stop=not start)

            def seg(i):
                g, part = i // 3, i % 3
                l_of, s_of, masked = ((0, 0, True), (1, 2, False), (1, 1, True))[part]
                pe.wait_ge(chi_ready, 1)
                pe.wait_ge(csq_lo, 1)
                pe.wait_ge(consts_ready, 1)
                for b in range(2):
                    take_bank(pe, ("seg", i), b)
                    h0 = HPG * g + 4 * b
                    o3 = X[:, b, :].rearrange("p (h l) -> p h l", h=4)
                    pe.matmul(o3, csq[:, s_of, :], sel[:, 1, h0:h0 + 4].unsqueeze(2).to_broadcast([2 * HEADS, 4, P]),
                              start=True, stop=False)
                    for h in range(4):
                        pe.matmul(X[:, b, h * P:(h + 1) * P], sel[:, 0, h0 + h:h0 + h + 1].to_broadcast([2 * HEADS, P]),
                                  csq[:, l_of, :], start=False, stop=False, skip_group_check=True)
                    if masked:
                        last = pe.matmul(o3, identb[:], cnegb[:].unsqueeze(1).to_broadcast([P, 4, P]),
                                         start=False, stop=True)
                    else:
                        last = add_nothing(b, start=False)
                    last.then_inc(bank_full[b], 1)

            def y_part(i):
                g, part = i // 3, i % 3
                pe.wait_ge(m_ready, i + 1)
                for b in range(M):
                    wait_kept(pe, ("turn_xs", g), b)
                if part < 2:
                    take_bank(pe, ("y_bank", 2 * g + part), 3)
                src = (0, 0, 1)[part]
                if part == 1:
                    add_nothing(3, start=True)
                for h in range(HPG):
                    last = pe.matmul(X[:, 3, h * HD:(h + 1) * HD], lm[:, h, :], xdt[:, src, h * HD:(h + 1) * HD],
                                     start=(part == 0), stop=(part == 0), skip_group_check=True)
                if part == 2:
                    last = add_nothing(3, start=False)
                last.then_inc(y_done if part == 1 else bank_full[3], 1)

            def turn_y(g):
                pe.wait_ge(y_normed, M * (g + 1))
                for e in range(2):
                    transposed(("turn_y", g), 2 + e, [yy[:, m, (2 * e + t) * P:(2 * e + t + 1) * P]
                                                      for t in range(2) for m in range(M)])

            PE = dict(turn_dt=turn_dt, turn_k=turn_k, turn_q=turn_q, scores=scores, turn_p=turn_p, pv=pv, decay_sums=decay_sums,
                      turn_u=turn_u, turn_xs=turn_xs, cb=cb, seg=seg, y_part=y_part, turn_y=turn_y)

            pe.wait_ge(ident_in, 16)
            for h in range(2):
                pe.wait_ge(x_in[h], 16)
                rows_transposed("x", xm, range(h * X_T // 2, (h + 1) * X_T // 2))

            def split_of(name):
                return lambda c: wait_kept(pe, (name, c), c % 4)

            for b in MIX_ORDER:
                kind, j = b
                n = START[b]
                if kind == "dt":
                    dt_products()
                    for name, arg in PE_STEPS.get(n, []):
                        step(name, arg)
                    continue
                if b == ("k", 0):
                    block_products(n, ACC[b], aT, ready=split_of("x"))
                elif kind == "att":
                    if j == 0:
                        wait_kept(pe, ("pv", KV - 1), 3)
                        wait_kept(pe, ("pv", KV - 1), 0)
                    block_products(n, ACC[b], bT)
                elif kind == "y":
                    wait_kept(pe, ("turn_y", GROUPS - 1), 2)
                    wait_kept(pe, ("turn_y", GROUPS - 1), 3)
                    block_products(n, ACC[b], cT)
                else:
                    block_products(n, ACC[b], aT)

            def turn_fresh(turn):
                pe.wait_ge(merged_ready, turn)
                for e in range(2):
                    for q in range(4):
                        last = pe.transpose(X[:, e, q * P:(q + 1) * P],
                                            yy[:, q % 2, (2 * e + q // 2) * P:(2 * e + q // 2 + 1) * P], ident[:])
                    last.then_inc(bank_full[e], 1)

            with pe.Fori(0, LOOP_Y) as i:
                def fresh(c):
                    if c == 5:
                        for e in range(2):
                            pe.wait_ge(bank_free[e], i + TURN[("merged", 0), e])
                        turn_fresh(i + 1)
                block_products(N_LOOP_Y, BLK_LOOP_Y, aT, 2 * CPB, 2, i, steps=False, between=fresh)
                block_products(N_LOOP_Y + CPB, BLK_LOOP_Y + 1, cT, 2 * CPB, 2, i, steps=False)

            def out_ready_(c):
                if c == 0:
                    wait_kept(pe, ("merged", LOOP_Y - 1), 0)
                    wait_kept(pe, ("merged", LOOP_Y - 1), 1)
                if c == 6:
                    wait_kept(pe, ("merged", LOOP_Y), 0)
                    wait_kept(pe, ("merged", LOOP_Y), 1)

            def last_merged(c):
                if c == 4:
                    for e in range(2):
                        take_bank(pe, ("merged", LOOP_Y), e)
                    turn_fresh(LOOP_Y + 1)

            for j in range(4):
                block_products(N_OUT + j * CPB, BLK_OUT + j, bT, steps=False,
                               ready=out_ready_ if j == 0 else None,
                               between=last_merged if j == 0 else None)
                if j == 2:
                    pe.wait_ge(mem_in, 16)
                    rows_transposed("mem", xm)

            def turn_heads(key, blk, first_bank):
                wait_block(pe, blk)
                for e in range(2):
                    transposed((key, 0), first_bank + e, [xqk[:, m, (2 * e + t) * P:(2 * e + t + 1) * P]
                                                          for t in range(2) for m in range(M)])

            def xscores():
                for b in range(2):
                    wait_kept(pe, ("xk", 0), b)
                    wait_kept(pe, ("xq", 0), 2 + b)
                for b in range(4):
                    take_bank(pe, ("xscores", 0), b)
                    m = b // 2
                    for h in range(2 * (b % 2), 2 * (b % 2) + 2):
                        last = pe.matmul(X[:, b, (h % 2) * SEQ:(h % 2 + 1) * SEQ], xqT[:, h, m * P:(m + 1) * P],
                                         xkT[:, h, :], start=True, stop=True)
                    last.then_inc(bank_full[b], 1)

            def turn_xp():
                pe.wait_ge(xp_ready, M)
                for t in range(M):
                    for e in range(2):
                        transposed((f"xturn_p{t}", 0), 2 * t + e,
                                   [xp[:, m, 2 * e + h, t * P:(t + 1) * P] for h in range(2) for m in range(M)])

            def beside_xk(c):
                if c in (4, 6):
                    pe.wait_ge(resid_ready, c // 2 - 1)
                    rows_transposed("h2", xm, range(4) if c == 4 else range(4, X_T))

            def beside_xq(c):
                if c == 2:
                    turn_heads("xk", BLK_XK, 0)

            def beside_xv(c):
                if c == 1:
                    turn_heads("xq", BLK_XQ, 2)
                if c == 3:
                    xscores()
                if c == 6:
                    turn_xp()

            block_products(N_XK, BLK_XK, aT, steps=False, ready=split_of("mem"), between=beside_xk)
            block_products(N_XQ, BLK_XQ, cT, steps=False, ready=split_of("h2"), between=beside_xq)
            block_products(N_XV, BLK_XV, aT, steps=False, between=beside_xv)
            for b in range(4):
                wait_kept(pe, (f"xturn_p{b // 2}", 0), b)
            wait_block(pe, BLK_XV)
            for e in range(2):
                take_bank(pe, ("xpv", 0), e)
                for h in range(2 * e, 2 * e + 2):
                    for t in range(M):
                        last = pe.matmul(X[:, e, (h % 2) * SEQ:(h % 2 + 1) * SEQ], xv[:, t, h * P:(h + 1) * P],
                                         xpT[:, t, h, :], start=(t == 0), stop=(t == 1))
                last.then_inc(bank_full[e], 1)
            for j in range(4):
                block_products(N_XO + 2 * j, BLK_XO + j, oT, k_tiles=XH, steps=False,
                               ready=(lambda c: wait_kept(pe, ("xpv", 0), c)) if j == 0 else None)
            for h in range(2):
                pe.wait_ge(resid_ready, 3 + h)
                rows_transposed("h3", xm, range(h * X_T // 2, (h + 1) * X_T // 2))

            def turn_hidden(i):
                pe.wait_ge(acc_free, i * 4 + 2 * BLK_FFN)
                for e in range(2):
                    pe.wait_ge(bank_free[e], i - 1 + TURN[("hidden", 0), e])
                    for q in range(4):
                        last = pe.transpose(X[:, e, q * P:(q + 1) * P],
                                            hid[:, q % 2, (2 * e + q // 2) * P:(2 * e + q // 2 + 1) * P], ident[:])
                    last.then_inc(bank_full[e], 1)

            block_products(N_FFN, BLK_FFN, aT, steps=False, ready=split_of("h3"))
            block_products(N_FFN + CPB, BLK_FFN + 1, aT, steps=False)
            with pe.Fori(1, FBLOCKS) as i:
                block_products(N_FFN, BLK_FFN, aT, 2 * CPB, 2, i, steps=False,
                               between=lambda c: turn_hidden(i) if c == 6 else None)
                block_products(N_FFN + CPB, BLK_FFN + 1, aT, 2 * CPB, 2, i, steps=False)

            def down(c, i, k, half, start, stop):
                pe.wait_ge(hq_lo, i * DOWN_UNROLL + k + 1)
                pe.wait_ge(lo_ready, N_DOWN + c + 1 + 2 * DOWN_UNROLL * i)
                s = (N_DOWN + c) % SPLIT
                banks = acc if half == 0 else X
                for j in (BLK_DOWN % 2, 1 - BLK_DOWN % 2):
                    if start and c == 0:
                        pe.wait_ge(acc_free, 2 * (BLK_DOWN - 1 if j == BLK_DOWN % 2 else BLK_DOWN))
                    for m in range(M):
                        for a, w in ((0, hi), (1, hi), (0, lo)):
                            last = pe.matmul(banks[:, 2 * j + m, :], hq[:, k, a, m * P:(m + 1) * P],
                                             w[:, s, j * COLS:(j + 1) * COLS],
                                             start=(start and a == 0 and w is hi), stop=(stop and w is lo),
                                             skip_group_check=True)
                        if stop:
                            last.then_inc(down_done, 1)
                if not stop:
                    last.then_inc(chunk_used, 1)

            for c in range(2 * DOWN_UNROLL):
                if c == 1:
                    turn_hidden(FBLOCKS)
                if c == DOWN_UNROLL:
                    for b in range(4):
                        take_bank(pe, ("down", 0), b)
                down(c, 0, c % DOWN_UNROLL, c // DOWN_UNROLL, c % DOWN_UNROLL == 0, False)
            with pe.Fori(1, DOWN_TURNS - 1) as i:
                for c in range(2 * DOWN_UNROLL):
                    down(c, i, c // 2, c % 2, False, False)
            for c in range(2 * DOWN_UNROLL):
                down(c, DOWN_TURNS - 1, c // 2, c % 2, False, c // 2 == DOWN_UNROLL - 1)

        @block.scalar
        def _(act):
            own = [0]

            def link(ins):
                own[0] += 1
                ins.then_inc(act_step, 1)
                act.wait_ge(act_step, own[0])

            def split(n, turns=0, i=0, size=KPC * COLS):
                slot = n % RAW
                act.wait_ge(raw_loaded[slot], 16 * (n // RAW + 1) + 16 * (turns // RAW) * i)
                if n >= SPLIT:
                    act.wait_ge(chunk_used, n - SPLIT + 1 + turns * i)
                act.activation(hi[:, n % SPLIT, 0:size], raw[:, slot, 0:size], ACT.Copy).then_inc(hi_ready, 1)

            def split_transposed(name, dst, gain, turns=range(X_T)):
                for j in turns:
                    b = j % 4
                    wait_bank(act, (name, j), b)
                    for k in range(2):
                        kt = 2 * j + k
                        ins = act.activation(dst[:, 0, kt, :], X[:, b, k * SEQ:(k + 1) * SEQ], ACT.Copy,
                                             scale=par[:, gain + kt:gain + kt + 1])
                    ins.then_inc(t_hi, 1)

            def squares(norm, src, m, scratch):
                link(act.activation(scratch, src, ACT.Square, accum_out=ssq[:, norm, m, 0:1]))

            def root(norm):
                if norm in (2, 4, 6):
                    act.wait_ge(sum_ready, norm // 2)
                    src = rstd[:, norm, :]
                else:
                    src = ssq[:, norm, :, 0]
                act.activation(rstd[:, norm, :], src, ACT.Sqrt, bias=eps[:], scale=1.0 / D).then_inc(root_ready, 1)

            def squares_x(_):
                for m in range(M):
                    squares(0, xm[:, m, :], m, mix[:, m, :])

            def root_x(_):
                root(0)

            def angles(_):
                act.wait_ge(angles_ready, 1)
                act.activation(rope[:, 0:2, :, :].rearrange("p a m f -> p (a m f)"),
                               ang[:, 4:6, :].rearrange("p a f -> p (a f)"), ACT.Sin).then_inc(rope_ready, 1)

            def keep(key, b, dst, k=2):
                wait_bank(act, key, b)
                act.activation(dst, X[:, b, :].rearrange("p (k t) -> p k t", k=k), ACT.Copy)\
                   .then_inc(bank_free[b], 1)

            def keep_k(_):
                for b in range(4):
                    keep(("turn_k", 0), b, kT[:, 2 * b:2 * b + 2, :])

            def keep_v(_):
                wait_norm(act, 0)
                act.wait_ge(chunk_used, end_of(("v", 0)))
                for m in range(M):
                    v = acc[:, 2 * (ACC[("v", 0)] % 2) + m, :].rearrange("p (g d) -> p g d", g=KV)
                    act.activation(vv[:, m, :, 0, :], v, ACT.Copy, scale=rstd[:, 0, m:m + 1])
                    act.activation(vv[:, m, :, 1, :], v, ACT.Copy, scale=rstd[:, 0, m:m + 1]).then_inc(acc_free, 1)

            def keep_q(b):
                for e in range(2):
                    keep(("turn_q", b), 2 + e, qT[:, 2 * e:2 * e + 2, :])

            def exponents(u):
                act.wait_ge(max_ready, u + 1)
                act.activation(esk[:], esk[:], ACT.Exp)
                for h in range(4):
                    act.activation(p0[:, h, :], p0[:, h, :], ACT.Exp, bias=nmx[:, h:h + 1],
                                   accum_out=rsum[:, h:h + 1])
                for h in range(4):
                    ins = act.activation(p1[:, h, 64:SEQ], p1[:, h, 64:SEQ], ACT.Exp, bias=nmx[:, 4 + h:5 + h],
                                         accum_out=rsum[:, 4 + h:5 + h])
                ins.then_inc(exp_ready, 1)

            def keep_p(u):
                for b in range(2):
                    keep(("turn_p", u), b, pT[:, b, :].unsqueeze(1), k=1)

            def keep_o(u):
                for m, b in ((0, 3), (1, 0)):
                    wait_bank(act, ("pv", u), b)
                    o = X[:, b, :].rearrange("p (a e t) -> p a e t", a=2, e=2)
                    for e in range(2):
                        r = slice(HD * e, HD * e + HD)
                        act.activation(bT[r, 0, 2 * u:2 * u + 2, m * P:(m + 1) * P], o[r, :, e, :], ACT.Copy)\
                           .then_inc(o_hi, 1)

            def keep_dt(_):
                act.wait_ge(chunk_used, START[("dt", 0)] + 1)
                act.activation(dtT[:], X[0:HEADS, 3, 0:SEQ], ACT.Copy).then_inc(dt_kept, 1)

            def delta_exp(_):
                act.wait_ge(sp_in, 1)
                act.activation(row[:, R_ALOG:R_ALOG + HEADS], row[:, R_ALOG:R_ALOG + HEADS], ACT.Exp)
                act.activation(sp[:, 2, :], sp[:, 1, :], ACT.Exp, scale=-1.0).then_inc(sp_exp, 1)

            def keep_sums(_):
                wait_bank(act, ("decay_sums", 0), 2)
                act.activation(csf[:, 0:2, :], X[0:2 * HEADS, 2, 0:SEQ].rearrange("p (m l) -> p m l", m=M),
                               ACT.Copy).then_inc(bank_free[2], 1)

            def sums_hi(_):
                act.wait_ge(cse_ready, 1)
                act.activation(chi[:], csf[:], ACT.Copy)
                act.activation(csq[0:HEADS, :, :], csf[0:HEADS, :, :], ACT.Copy).then_inc(chi_ready, 1)

            def keep_u(i):
                b = CONV_UNITS[i]
                act.wait_ge(chunk_used, end_of(b))
                for m in range(M):
                    act.activation(uc[:, m * COLS:(m + 1) * COLS], acc[:, 2 * (ACC[b] % 2) + m, :], ACT.Copy,
                                   scale=rstd[:, 0, m:m + 1]).then_inc(acc_free, 1)

            def last_tap(i):
                t0 = 16 + 4 * i if i < 2 else 4 * (i - 2)
                for e in range(2):
                    wait_bank(act, ("turn_u", i), e)
                for c in range(4):
                    act.activation(uc[:, c * SEQ:(c + 1) * SEQ], X[:, c // 2, (c % 2) * SEQ:(c % 2 + 1) * SEQ],
                                   ACT.Identity, bias=par[:, CONV_B + t0 + c:CONV_B + t0 + c + 1],
                                   scale=par[:, CONV_W + 72 + t0 + c:CONV_W + 73 + t0 + c]).then_inc(tap_ready, 1)

            def silu(i):
                for e in range(2):
                    wait_kept(act, ("turn_u", i), e)
                dst = uc[:] if i >= 2 else bcT[:, i, :, :].rearrange("p g t -> p (g t)")
                act.activation(dst, uc[:], ACT.Silu).then_inc(silu_ready, 1)

            def keep_xs(g):
                for m in range(M):
                    wait_bank(act, ("turn_xs", g), m)
                    act.activation(xs[:, m, :], X[:, m, :], ACT.Copy).then_inc(xs_ready, 1)

            def keep_z(g):
                act.wait_ge(chunk_used, end_of(("z", g)))
                for m in range(M):
                    act.activation(sz[:, m, :], acc[:, 2 * (ACC[("z", g)] % 2) + m, :], ACT.Silu,
                                   scale=rstd[:, 0, m:m + 1]).then_inc(acc_free, 1)

            def keep_cb(g):
                wait_bank(act, ("cb", g), 2)
                act.activation(cbs[:], X[:, 2, 0:3 * P], ACT.Copy).then_inc(bank_free[2], 1)

            def decay(i):
                for b in range(2):
                    wait_bank(act, ("seg", i), b)
                if i:
                    g, part = (i - 1) // 3, (i - 1) % 3
                    if part == 1:
                        act.wait_ge(y_done, g + 1)
                    else:
                        wait_bank(act, ("y_bank", 2 * g + (part == 2)), 3)
                for b in range(2):
                    act.activation(lm[:, 4 * b:4 * b + 4, :], X[:, b, :].rearrange("p (h l) -> p h l", h=4),
                                   ACT.Exp).then_inc(bank_free[b], 1)

            def gate_root(i):
                m = i % 2
                act.wait_ge(y_gated, i + 1)
                link(act.activation(xs[:, m, :], yy[:, m, :], ACT.Square, accum_out=ysq[:, m:m + 1]))
                act.activation(yrs[:, m:m + 1], ysq[:, m:m + 1], ACT.Sqrt, bias=eps[:], scale=1.0 / COLS)\
                   .then_inc(y_root, 1)

            def keep_y(g):
                for e in range(2):
                    wait_bank(act, ("turn_y", g), 2 + e)
                    for k in range(2):
                        kt = 4 * g + 2 * e + k
                        ins = act.activation(cT[:, 0, kt, :], X[:, 2 + e, k * SEQ:(k + 1) * SEQ], ACT.Copy,
                                             scale=par[:, G_SSD + kt:G_SSD + kt + 1])
                    ins.then_inc(yT_hi, 1)

            def sigmoid(b):
                kind, j = b
                act.wait_ge(chunk_used, end_of(b))
                if kind == "gs" or j:
                    wait_block(act, ACC[("att", 3 if kind == "gs" else j - 1)])
                for m in range(M):
                    act.activation(gate[:, m, :], acc[:, 2 * (ACC[b] % 2) + m, :], ACT.Sigmoid,
                                   scale=rstd[:, 0, m:m + 1]).then_inc(acc_free, 1)

            STEPS = dict(squares_x=squares_x, root_x=root_x, angles=angles, keep_dt=keep_dt, keep_k=keep_k, keep_v=keep_v, keep_q=keep_q, exponents=exponents, keep_p=keep_p,
                         keep_o=keep_o, delta_exp=delta_exp, keep_sums=keep_sums, sums_hi=sums_hi, keep_u=keep_u,
                         last_tap=last_tap, silu=silu, keep_xs=keep_xs, keep_z=keep_z, keep_cb=keep_cb,
                         decay=decay, gate_root=gate_root, keep_y=keep_y, sigmoid=sigmoid)

            for h in range(2):
                act.dma_start(xm[:, :, h * D // 2:(h + 1) * D // 2],
                              x[:, :, h * D // 2:(h + 1) * D // 2].rearrange("b (m p) d -> p (b m) d", p=P))\
                   .then_inc(x_in[h], 16)
            act.wait_ge(consts_in, 96)
            for h in range(2):
                split_transposed("x", aT, G_MIX, range(h * X_T // 2, (h + 1) * X_T // 2))
                for n in range(h * AHEAD // 2, (h + 1) * AHEAD // 2):
                    split(n)
            act.activation(identb[:], ctmp[:, C_IDENT:C_IDENT + P], ACT.Copy)
            act.activation(cnegb[:], ctmp[:, C_CNEG:C_CNEG + P], ACT.Copy)
            for e in range(2):
                act.activation(sel[:, e, :], ctmp[0:2 * HEADS, C_SEL:C_SEL + HEADS], ACT.Copy, scale=1.0 - 2 * e)
            act.activation(eps[:], ctmp[:, C_EPS:C_EPS + 1], ACT.Copy).then_inc(consts_ready, 1)
            act.wait_ge(consts_ready, 1)
            for h in range(2):
                act.wait_ge(x_in[h], 16)
            for n in range(AHEAD, N_LOOP_Y):
                split(n, size=KT * HEADS if n == START[("dt", 0)] else KPC * COLS)
                for name, arg in ACT_STEPS.get(n, []):
                    STEPS[name](arg)

            def keep_merged(turn, k_at):
                for e in range(2):
                    act.wait_ge(bank_full[e], turn + TURN[("merged", 0), e] + 1)
                    act.activation(bT[:, 0, k_at(2 * e), :], X[:, e, :].rearrange("p (k t) -> p k t", k=2),
                                   ACT.Copy).then_inc(merged_hi, 1)

            with act.Fori(0, LOOP_Y) as i:
                for c in range(2 * CPB):
                    split(N_LOOP_Y + c, 2 * CPB, i)
                    if c == CPB + 1:
                        keep_merged(i, lambda k: bass.ds(i * 4 + k, 2))
                    if c == CPB + 3:
                        act.wait_ge(chunk_used, N_LOOP_Y + CPB + i * 2 * CPB)
                        act.wait_ge(acc_free, i * 4 + 2 * BLK_LOOP_Y)
                        for m in range(M):
                            act.activation(gate[:, m, :], acc[:, 2 * (BLK_LOOP_Y % 2) + m, :], ACT.Sigmoid,
                                           scale=rstd[:, 0, m:m + 1]).then_inc(acc_free, 1)

            def square_projected(norm, blk, n_end, j):
                act.wait_ge(chunk_used, n_end)
                if norm > 2 or j:
                    act.wait_ge(block_sq, 8 * (norm // 2 - 1) + 2 * j)
                for m in range(M):
                    act.activation(gate[:, m, :], acc[:, 2 * (blk % 2) + m, :], ACT.Square,
                                   accum_out=ssq[:, norm, m, j:j + 1]).then_inc(block_sq, 1)

            def scaled_heads(dst, blk, n_end, norm):
                wait_norm(act, norm)
                act.wait_ge(chunk_used, n_end)
                for m in range(M):
                    act.activation(dst[:, m, :], acc[:, 2 * (blk % 2) + m, :], ACT.Copy,
                                   scale=rstd[:, norm, m:m + 1]).then_inc(acc_free, 1)

            for n in range(N_OUT, N_FFN):
                split(n)
                if n == N_OUT + 8:
                    keep_merged(LOOP_Y, lambda k: slice(LOOP_Y * 4 + k, LOOP_Y * 4 + k + 2))
                for j in range(4):
                    if n == N_OUT + (j + 1) * CPB + 3:
                        square_projected(2, BLK_OUT + j, n - 3, j)
                    if n == N_XO + (j + 1) * 2 + 3:
                        square_projected(4, BLK_XO + j, n - 3, j)
                if n in (N_OUT + 14, N_OUT + 16):
                    act.wait_ge(mem_in, 16)
                    squares(1, xm[:, (n - N_OUT) // 2 - 7, :], (n - N_OUT) // 2 - 7, junk[:])
                if n == N_OUT + 17:
                    root(1)
                if n == N_OUT + 3 * CPB + 3:
                    split_transposed("mem", aT, G_MEM)
                if n == N_XK + 3:
                    root(2)
                if n in (N_XK + 6, N_XK + 7):
                    act.wait_ge(resid_ready, 2)
                    squares(3, xm[:, n - N_XK - 6, :], n - N_XK - 6, mix[:, n - N_XK - 6, :])
                if n == N_XK + 8:
                    split_transposed("h2", cT, G_XA, range(4))
                    root(3)
                if n == N_XK + 10:
                    split_transposed("h2", cT, G_XA, range(4, X_T))
                if n == N_XQ + 3:
                    scaled_heads(xqk, BLK_XK, N_XQ, 1)
                if n == N_XQ + 6:
                    for e in range(2):
                        keep(("xk", 0), e, xkT[:, 2 * e:2 * e + 2, :])
                if n == N_XV + 3:
                    scaled_heads(xqk, BLK_XQ, N_XV, 3)
                if n == N_XV + 5:
                    keep(("xq", 0), 2, xqT[:, 0:2, :])
                if n == N_XV + 7:
                    for b in range(4):
                        act.wait_ge(xmax_ready, b + 1)
                        for h in range(2):
                            q = 2 * b + h
                            ins = act.activation(xp[:, b // 2, q % 4, :], X[:, b, h * SEQ:(h + 1) * SEQ], ACT.Exp,
                                                 bias=nmx[:, q:q + 1], scale=X_SCALE, accum_out=rsum[:, q:q + 1])
                        ins.then_inc(bank_free[b], 1)
                if n == N_XO + 2:
                    for e in range(2):
                        keep(("xturn_p0", 0), e, xpT[:, 0, 2 * e:2 * e + 2, :])
                if n == N_XO + 3:
                    scaled_heads(xv, BLK_XV, N_XO, 1)
                    for e in range(2):
                        wait_bank(act, ("xpv", 0), e)
                        act.activation(oT[:, 0, 2 * e:2 * e + 2, :], X[:, e, :].rearrange("p (k t) -> p k t", k=2),
                                       ACT.Copy).then_inc(xo_hi, 1)
            for n in range(N_FFN, N_FFN + AHEAD):
                split(n)
                if n == N_FFN + 1:
                    square_projected(4, BLK_XO + 2, N_XO + 6, 2)
            square_projected(4, BLK_XO + 3, N_FFN, 3)
            root(4)
            split_transposed("h3", aT, G_FFN)

            def silu_of(i, more):
                act.wait_ge(chunk_used, N_FFN + CPB + more * 2 * CPB)
                for m in range(M):
                    act.activation(hid[:, m, :], acc[:, 2 * (BLK_FFN % 2) + m, :], ACT.Silu,
                                   scale=rstd[:, 5, m:m + 1]).then_inc(acc_free, 1)

            def keep_hidden(i):
                act.wait_ge(bank_full[0], TURN[("hidden", 0), 0] + 1 + i)
                k_tiles = slice(4 * i, 4 * i + 2) if isinstance(i, int) else bass.ds(i * 4, 2)
                act.activation(hT[:, k_tiles, :], X[:, 0, :].rearrange("p (k t) -> p k t", k=2), ACT.Copy)\
                   .then_inc(bank_free[0], 1)

            for n in range(N_FFN + AHEAD, N_FFN + 2 * CPB):
                split(n)
                if n in (N_FFN + 5, N_FFN + 6):
                    act.wait_ge(resid_ready, 4)
                    squares(5, xm[:, n - N_FFN - 5, :], n - N_FFN - 5, mix[:, n - N_FFN - 5, :])
                if n == N_FFN + 7:
                    root(5)
                if n == N_FFN + CPB + 3:
                    wait_norm(act, 5)
                    silu_of(0, 0)
            with act.Fori(1, FBLOCKS) as i:
                for c in range(2 * CPB):
                    split(N_FFN + c, 2 * CPB, i)
                    if c == CPB + 2:
                        keep_hidden(i - 1)
                        act.wait_ge(bank_full[1], i + TURN[("hidden", 0), 1])
                    if c == CPB + 3:
                        silu_of(i, i)

            def split_hidden(i, k):
                if not (isinstance(i, int) and i == 0):
                    act.wait_ge(chunk_used, N_DOWN + DOWN_UNROLL + k + 1 + (i - 1) * 2 * DOWN_UNROLL)
                kt = bass.ds(i * DOWN_UNROLL + k, 1) if not isinstance(i, int) else slice(k, k + 1)
                act.activation(hq[:, k, 0:1, :], hT[:, kt, :], ACT.Copy).then_inc(hq_hi, 1)

            for k in range(DOWN_UNROLL):
                split_hidden(0, k)
            for c in range(2 * DOWN_UNROLL):
                split(N_DOWN + c)
                if c == DOWN_UNROLL:
                    keep_hidden(FBLOCKS - 1)
            for e in range(2):
                act.wait_ge(bank_free[e], TURN[("hidden", 0), e] + FBLOCKS)
            with act.Fori(1, DOWN_TURNS) as i:
                for k in range(DOWN_UNROLL):
                    split_hidden(i, k)
                    for c in (2 * k, 2 * k + 1):
                        split(N_DOWN + c, 2 * DOWN_UNROLL, i)
            for q in range(2):
                act.wait_ge(block_sq, 16 + 4 * q)
                for b in range(4):
                    act.wait_ge(down_done, 4 * q + b + 1)
                    j, m = 2 * q + (b // 2 + BLK_DOWN) % 2, b % 2
                    src = (acc if q == 0 else X)[:, 2 * (j % 2) + m, :]
                    act.activation(squared[:, b, :], src, ACT.Square, accum_out=ssq[:, 6, m, j:j + 1])\
                       .then_inc(block_sq, 1)
            root(6)

        @block.vector
        def _(dve):
            own = [0]

            def link(ins):
                own[0] += 1
                ins.then_inc(dve_step, 1)
                dve.wait_ge(dve_step, own[0])

            def f32(ap):
                return ap.bitcast(F32)

            def split(n, turns=0, i=0, size=KPC * COLS):
                dve.wait_ge(hi_ready, n + 1 + turns * i)
                s = n % SPLIT
                dve.tensor_tensor(lo[:, s, 0:size], raw[:, n % RAW, 0:size], f32(hi[:, s, 0:size]),
                                  ALU.subtract).then_inc(lo_ready, 1)

            def split_transposed(name, turn, dst, gain, turns=range(X_T)):
                for j in turns:
                    b = j % 4
                    dve.wait_ge(t_hi, turn * X_T + j + 1)
                    for k in range(2):
                        kt = 2 * j + k
                        ins = dve.scalar_tensor_tensor(out=dst[:, 1, kt, :], in0=X[:, b, k * SEQ:(k + 1) * SEQ],
                                                       scalar=par[:, gain + kt:gain + kt + 1],
                                                       in1=f32(dst[:, 0, kt, :]), op0=ALU.mult, op1=ALU.subtract)
                    ins.then_inc(bank_free[b], 1)

            def factor(norm):
                dve.wait_ge(root_ready, norm + 1)
                return dve.reciprocal(rstd[:, norm, :], rstd[:, norm, :])

            def sum_blocks(norm):
                dve.wait_ge(block_sq, 8 * (norm // 2))
                dve.tensor_reduce(rstd[:, norm, :], ssq[:, norm, :, :], AX.X, ALU.add).then_inc(sum_ready, 1)

            def rotate(blk, m, dsts):
                a = acc[:, 2 * (blk % 2) + m, :]
                sw = swapped[:].rearrange("p (h e r) -> p h e r", e=2, r=32)
                a4 = a.rearrange("p (h e r) -> p h e r", e=2, r=32)
                for e in range(2):
                    t = rope[:, 2 - e, m, :].unsqueeze(1).to_broadcast([P, 8, 32])
                    dve.tensor_tensor(sw[:, :, e, :], a4[:, :, 1 - e, :], t, ALU.mult)
                dve.tensor_tensor(qs[:, m, :].rearrange("p (h r) -> p h r", r=32),
                                  a.rearrange("p (h r) -> p h r", r=32),
                                  rope[:, 0, m, :].unsqueeze(1).to_broadcast([P, 16, 32]), ALU.mult)\
                   .then_inc(acc_free, 1)
                dve.wait_ge(acc_free, 2 * blk + m + 1)
                for dst in dsts:
                    ins = dve.tensor_tensor(dst, qs[:, m, :].rearrange("p (h d) -> p h d", d=HD),
                                            swapped[:].rearrange("p (h d) -> p h d", d=HD), ALU.add)
                return ins

            def rope_k(_):
                dve.wait_ge(chunk_used, end_of(("k", 0)))
                link(rotate(ACC[("k", 0)], 0, [kk[:, 0, :, e, :] for e in range(2)]))
                rotate(ACC[("k", 0)], 1, [kk[:, 1, :, e, :] for e in range(2)]).then_inc(k_roped, 1)

            def rope_q(b):
                dve.wait_ge(chunk_used, end_of(("q", b)))
                blk = ACC[("q", b)]
                link(rotate(blk, 0, [qs[:, 0, :].rearrange("p (h d) -> p h d", d=HD)]))
                rotate(blk, 1, [qs[:, 1, :].rearrange("p (h d) -> p h d", d=HD)]).then_inc(q_roped, 1)

            def maxima(u):
                h0 = 4 * u
                wait_bank(dve, ("scores", u), 0)
                dve.scalar_tensor_tensor(out=p0[:], in0=X[:, 0, :].rearrange("p (h k) -> p h k", h=4),
                                         scalar=ATT_SCALE, in1=am0[:].unsqueeze(1).to_broadcast([P, 4, P]),
                                         op0=ALU.mult, op1=ALU.add).then_inc(bank_free[0], 1)
                for b in (1, 2):
                    wait_bank(dve, ("scores", u), b)
                    dve.scalar_tensor_tensor(out=p1[:, 2 * b - 2:2 * b, 64:SEQ],
                                             in0=X[:, b, :].rearrange("p (h k) -> p h k", h=2)[:, :, 64:SEQ],
                                             scalar=ATT_SCALE, in1=am1[:].unsqueeze(1).to_broadcast([P, 2, 192]),
                                             op0=ALU.mult, op1=ALU.add).then_inc(bank_free[b], 1)
                wait_kept(dve, ("scores", u), 2)
                dve.tensor_reduce(mx[:, 0:4], p0[:], AX.X, ALU.max)
                link(dve.tensor_reduce(mx[:, 4:8], p1[:, :, 64:SEQ], AX.X, ALU.max))
                sink = row[:, R_SINK + h0:R_SINK + h0 + 4].unsqueeze(1).to_broadcast([P, 2, 4])
                mx2, esk2 = (t[:].rearrange("p (m h) -> p m h", m=M) for t in (mx, esk))
                link(dve.tensor_tensor(mx2, mx2, sink, ALU.max))
                dve.tensor_scalar(nmx[:], mx[:], -1.0, None, ALU.mult)
                dve.tensor_tensor(esk2, sink, mx2, ALU.subtract).then_inc(max_ready, 1)

            def probabilities(u):
                dve.wait_ge(exp_ready, u + 1)
                link(dve.tensor_tensor(rsum[:], rsum[:], esk[:], ALU.add))
                link(dve.reciprocal(rsum[:], rsum[:]))
                dve.tensor_tensor(p0[:], p0[:], rsum[:, 0:4].unsqueeze(2).to_broadcast([P, 4, P]), ALU.mult)
                dve.tensor_tensor(p1[:, :, 64:SEQ], p1[:, :, 64:SEQ],
                                  rsum[:, 4:8].unsqueeze(2).to_broadcast([P, 4, 192]), ALU.mult)\
                   .then_inc(probs_ready, 1)

            def keep_p(u):
                wait_bank(dve, ("turn_p", u), 2)
                dve.tensor_copy(pT[:, 2, :], X[:, 2, :]).then_inc(bank_free[2], 1)

            def keep_o(u):
                for m, b in ((0, 3), (1, 0)):
                    o = X[:, b, :].rearrange("p (a e t) -> p a e t", a=2, e=2)
                    dve.wait_ge(o_hi, 4 * u + 2 * m + 2)
                    for e in range(2):
                        r = slice(HD * e, HD * e + HD)
                        t = slice(m * P, (m + 1) * P)
                        ins = dve.tensor_tensor(bT[r, 1, 2 * u:2 * u + 2, t], o[r, :, e, :],
                                                f32(bT[r, 0, 2 * u:2 * u + 2, t]), ALU.subtract)
                    ins.then_inc(bank_free[b], 1)

            def delta_in(_):
                t, a = sp[:, 0, :], sp[:, 1, :]
                wait_bank(dve, ("dt", 0), 3)
                for m in range(M):
                    h = slice(m * HEADS, (m + 1) * HEADS)
                    ins = dve.scalar_tensor_tensor(out=t[:, h], in0=X[:, 3, h], scalar=rstd[:, 0, m:m + 1],
                                                   in1=row[:, R_DTB:R_DTB + HEADS], op0=ALU.mult, op1=ALU.add)
                ins.then_inc(bank_free[3], 1)
                wait_kept(dve, ("dt", 0), 3)
                link(dve.tensor_scalar(a, t, -1.0, None, ALU.mult))
                dve.tensor_tensor(a, a, t, ALU.max).then_inc(sp_in, 1)

            def delta_series(_):
                u, z, z2, q = (sp[:, k, :] for k in range(2, 6))
                dve.wait_ge(sp_exp, 1)
                link(dve.tensor_scalar(z2, u, 2.0, None, ALU.add))
                link(dve.reciprocal(z2, z2))
                link(dve.tensor_tensor(z, u, z2, ALU.mult))
                link(dve.tensor_tensor(z2, z, z, ALU.mult))
                link(dve.tensor_scalar(q, z2, 1.0 / 15, None, ALU.mult))
                for k in (13, 11, 9, 7, 5, 3):
                    link(dve.scalar_tensor_tensor(out=q, in0=q, scalar=1.0 / k, in1=z2, op0=ALU.add, op1=ALU.mult))

            def delta_out(_):
                t, a, z, q = sp[:, 0, :], sp[:, 1, :], sp[:, 3, :], sp[:, 5, :]
                link(dve.scalar_tensor_tensor(out=q, in0=q, scalar=1.0, in1=z, op0=ALU.add, op1=ALU.mult))
                link(dve.tensor_scalar(a, t, 0.0, None, ALU.max))
                d = dt[:].rearrange("p m h -> p (m h)")
                link(dve.scalar_tensor_tensor(out=d, in0=q, scalar=2.0, in1=a, op0=ALU.mult, op1=ALU.add))
                for e in range(2):
                    ins = dve.scalar_tensor_tensor(
                        out=da2[:, :, e, :], in0=dt[:], scalar=-1.0,
                        in1=row[:, R_ALOG:R_ALOG + HEADS].unsqueeze(1).to_broadcast([P, M, HEADS]),
                        op0=ALU.mult, op1=ALU.mult)
                ins.then_inc(da_ready, 1)

            def keep_sums(_):
                wait_kept(dve, ("decay_sums", 0), 2)
                dve.tensor_scalar(csf[:, 2, :], csf[:, 0, :], csf[:, 0, P - 1:P], None, ALU.subtract)\
                   .then_inc(cse_ready, 1)

            def sums_lo(_):
                dve.wait_ge(chi_ready, 1)
                r = slice(HEADS, 2 * HEADS)
                dve.tensor_tensor(csq[r, :, :], csf[r, :, :], f32(chi[r, :, :]), ALU.subtract).then_inc(csq_lo, 1)

            def taps(i):
                t0 = 16 + 4 * i if i < 2 else 4 * (i - 2)
                for e in range(2):
                    dve.wait_ge(tap_ready, 4 * i + 2 * e + 2)
                    for s in (1, 2, 3):
                        for c in (2 * e, 2 * e + 1):
                            w = CONV_W + 24 * (3 - s) + t0 + c
                            o = uc[:, c * SEQ + s:(c + 1) * SEQ]
                            ins = dve.scalar_tensor_tensor(out=o, in0=X[:, e, (c % 2) * SEQ:(c % 2 + 1) * SEQ - s],
                                                           scalar=par[:, w:w + 1], in1=o, op0=ALU.mult, op1=ALU.add)
                        if s < 3:
                            link(ins)
                        else:
                            ins.then_inc(bank_free[e], 1)

            def keep_xs(g):
                for m in range(M):
                    dve.wait_ge(xs_ready, 2 * g + m + 1)
                    dve.tensor_tensor(xdt[:, m, :].rearrange("p (h d) -> p h d", d=HD),
                                      X[:, m, :].rearrange("p (h d) -> p h d", d=HD),
                                      dt[:, m, HPG * g:HPG * (g + 1)].unsqueeze(2).to_broadcast([P, HPG, HD]),
                                      ALU.mult).then_inc(bank_free[m], 1)

            def decay(i):
                g, part = i // 3, i % 3
                if part == 0:
                    wait_kept(dve, ("cb", g), 2)
                for b in range(2):
                    wait_kept(dve, ("seg", i), b)
                c = cbs[:, part * P:(part + 1) * P].unsqueeze(1).to_broadcast([P, HPG, P])
                dve.tensor_tensor(lm[:], lm[:], c, ALU.mult).then_inc(m_ready, 1)

            def gate_y(i):
                g, m = i // 2, i % 2
                y, h3 = yy[:, m, :], (lambda ap: ap.rearrange("p (h d) -> p h d", d=HD))
                skip = row[:, R_DSKIP + HPG * g:R_DSKIP + HPG * (g + 1)].unsqueeze(2).to_broadcast([P, HPG, HD])
                link(dve.tensor_tensor(h3(y), h3(xs[:, m, :]), skip, ALU.mult))
                wait_bank(dve, ("y_bank", i), 3)
                dve.tensor_tensor(y, X[:, 3, :], y, ALU.add).then_inc(bank_free[3], 1)
                wait_kept(dve, ("y_bank", i), 3)
                wait_block(dve, ACC[("z", g)])
                dve.tensor_tensor(y, y, sz[:, m, :], ALU.mult).then_inc(y_gated, 1)

            def norm_y(i):
                m = i % 2
                y, r = yy[:, m, :], yrs[:, m:m + 1]
                dve.wait_ge(y_root, i + 1)
                link(dve.reciprocal(r, r))
                dve.tensor_scalar(y, y, r, None, ALU.mult).then_inc(y_normed, 1)

            def keep_y(g):
                for e in range(2):
                    dve.wait_ge(yT_hi, 2 * g + e + 1)
                    for k in range(2):
                        kt = 4 * g + 2 * e + k
                        ins = dve.scalar_tensor_tensor(out=cT[:, 1, kt, :], in0=X[:, 2 + e, k * SEQ:(k + 1) * SEQ],
                                                       scalar=par[:, G_SSD + kt:G_SSD + kt + 1],
                                                       in1=f32(cT[:, 0, kt, :]), op0=ALU.mult, op1=ALU.subtract)
                    ins.then_inc(bank_free[2 + e], 1)

            def merge_att(j):
                b = ("att", j)
                dve.wait_ge(chunk_used, end_of(b))
                wait_block(dve, ACC[b] - 1)
                for m in range(M):
                    dve.tensor_tensor(xm[:, m, j * COLS:(j + 1) * COLS], acc[:, 2 * (ACC[b] % 2) + m, :],
                                      gate[:, m, :], ALU.mult).then_inc(acc_free, 1)

            def angles(_):
                dve.wait_ge(pos_in, 16)
                dve.wait_ge(consts_in, 48)
                link(dve.tensor_copy(ysq[:], pos[:]))
                for m in range(M):
                    ins = dve.tensor_scalar(ang[:, 0, m * 32:(m + 1) * 32], ctmp[:, C_FREQ:C_FREQ + 32],
                                            ysq[:, m:m + 1], None, ALU.mult)
                link(ins)
                pi_a = 6.28125
                pi_b = float(np.float32(np.round((2 * np.pi - pi_a) * 2 ** 20) / 2 ** 20))
                pi_c = float(np.float32(2 * np.pi - pi_a - pi_b))
                for dst, quarter in ((4, 0.25), (5, 0.0)):
                    r, t = ang[:, dst, :], ang[:, 1, :]
                    link(dve.tensor_scalar(t, ang[:, 0, :], 1 / (2 * np.pi), quarter, ALU.mult, ALU.add))
                    link(dve.tensor_scalar(t, t, 12582912.0, None, ALU.add))
                    link(dve.tensor_scalar(t, t, -12582912.0, None, ALU.add))
                    link(dve.scalar_tensor_tensor(out=r, in0=t, scalar=-pi_a, in1=ang[:, 0, :], op0=ALU.mult,
                                                  op1=ALU.add))
                    for part in (pi_b, pi_c):
                        link(dve.scalar_tensor_tensor(out=r, in0=t, scalar=-part, in1=r, op0=ALU.mult, op1=ALU.add))
                    link(dve.tensor_scalar(r, r, quarter * 2 * np.pi, 3.1415925, ALU.add, ALU.min))
                    ins = dve.tensor_scalar(r, r, -3.1415925, None, ALU.max)
                    link(ins) if dst == 4 else ins.then_inc(angles_ready, 1)

            def norm_x(_):
                factor(0).then_inc(norm_ready, 1)
                wait_norm(dve, 0)
                dve.wait_ge(rope_ready, 1)
                link(dve.tensor_scalar(rope[:, 2, :, :], rope[:, 1, :, :], -1.0, None, ALU.mult))
                for m in range(M):
                    link(dve.tensor_scalar(rope[:, :, m, :], rope[:, :, m, :], rstd[:, 0, m:m + 1], None, ALU.mult))
                link(dve.memset(p1[:, :, 0:64], 0.0))

            STEPS = dict(angles=angles, norm_x=norm_x, rope_k=rope_k, rope_q=rope_q, maxima=maxima, probabilities=probabilities, keep_p=keep_p,
                         keep_o=keep_o, delta_in=delta_in, delta_series=delta_series, delta_out=delta_out,
                         keep_sums=keep_sums, sums_lo=sums_lo, taps=taps, keep_xs=keep_xs, decay=decay,
                         gate_y=gate_y, norm_y=norm_y, keep_y=keep_y, merge_att=merge_att)

            dve.wait_ge(consts_in, 96)
            for h in range(2):
                split_transposed("x", 0, aT, G_MIX, range(h * X_T // 2, (h + 1) * X_T // 2))
                for n in range(h * AHEAD // 2, (h + 1) * AHEAD // 2):
                    split(n)
            for n in range(AHEAD, N_LOOP_Y):
                split(n, size=KT * HEADS if n == START[("dt", 0)] else KPC * COLS)
                for name, arg in DVE_STEPS.get(n, []):
                    STEPS[name](arg)

            def merge_y(turn, cols):
                blk, n_end = BLK_LOOP_Y - 1, N_LOOP_Y
                dve.wait_ge(chunk_used, n_end + turn * 2 * CPB)
                wait_block(dve, blk - 1, 4 * turn)
                for m in range(M):
                    dve.tensor_tensor(yy[:, m, :], acc[:, 2 * (blk % 2) + m, :], gate[:, m, :], ALU.mult)\
                       .then_inc(acc_free, 1)
                wait_block(dve, blk, 4 * turn)
                dve.tensor_tensor(yy[:, 0, :], yy[:, 0, :], xm[:, 0, cols], ALU.add)
                dve.tensor_tensor(yy[:, 1, :], yy[:, 1, :], xm[:, 1, cols], ALU.add).then_inc(merged_ready, 1)

            def keep_merged(turn, k_at):
                for e in range(2):
                    dve.wait_ge(merged_hi, 2 * turn + e + 1)
                    dve.tensor_tensor(bT[:, 1, k_at(2 * e), :], X[:, e, :].rearrange("p (k t) -> p k t", k=2),
                                      f32(bT[:, 0, k_at(2 * e), :]), ALU.subtract).then_inc(bank_free[e], 1)

            with dve.Fori(0, LOOP_Y) as i:
                for c in range(2 * CPB):
                    split(N_LOOP_Y + c, 2 * CPB, i)
                    if c == 3:
                        merge_y(i, bass.ds(i * COLS, COLS))
                    if c == CPB + 1:
                        keep_merged(i, lambda k: bass.ds(i * 4 + k, 2))

            def keep_projected(norm, blk, j, gain):
                dve.wait_ge(gain_in, 16 * (norm // 2))
                for m in range(M):
                    dve.wait_ge(block_sq, 8 * (norm // 2 - 1) + 2 * j + m + 1)
                    dve.tensor_tensor(mix[:, m, j * COLS:(j + 1) * COLS], acc[:, 2 * (blk % 2) + m, :],
                                      gain[:, j * COLS:(j + 1) * COLS], ALU.mult).then_inc(acc_free, 1)

            def add_residual(norm, h, residual):
                cols = slice(h * D // 2, (h + 1) * D // 2)
                for m in range(M):
                    ins = dve.scalar_tensor_tensor(out=xm[:, m, cols], in0=mix[:, m, cols],
                                                   scalar=rstd[:, norm, m:m + 1], in1=residual[:, m, cols],
                                                   op0=ALU.mult, op1=ALU.add)
                ins.then_inc(resid_ready, 1)

            for n in range(N_OUT, N_FFN):
                split(n)
                if n == N_OUT + 3:
                    merge_y(LOOP_Y, slice(LOOP_Y * COLS, (LOOP_Y + 1) * COLS))
                if n == N_OUT + 8:
                    keep_merged(LOOP_Y, lambda k: slice(LOOP_Y * 4 + k, LOOP_Y * 4 + k + 2))
                for j in range(4):
                    if n == N_OUT + (j + 1) * CPB + 3:
                        keep_projected(2, BLK_OUT + j, j, gb)
                    if n == N_XO + (j + 1) * 2 + 3:
                        keep_projected(4, BLK_XO + j, j, gx)
                if n == N_OUT + 18:
                    factor(1).then_inc(norm_ready, 1)
                if n == N_OUT + 3 * CPB + 3:
                    split_transposed("mem", 1, aT, G_MEM)
                if n == N_XK + 3:
                    sum_blocks(2)
                    dve.wait_ge(bank_full[3], TURN[("mem", X_T - 1), 3] + 1)
                    dve.wait_ge(x_again, 16)
                if n == N_XK + 4:
                    link(factor(2))
                    wait_block(dve, BLK_OUT + 3)
                    add_residual(2, 0, xr)
                if n == N_XK + 5:
                    add_residual(2, 1, xr)
                if n == N_XK + 8:
                    split_transposed("h2", 2, cT, G_XA, range(4))
                if n == N_XK + 9:
                    factor(3).then_inc(norm_ready, 1)
                if n == N_XK + 10:
                    split_transposed("h2", 2, cT, G_XA, range(4, X_T))
                if n == N_XV + 5:
                    wait_bank(dve, ("xq", 0), 3)
                    dve.tensor_copy(xqT[:, 2:4, :], X[:, 3, :].rearrange("p (k t) -> p k t", k=2))\
                       .then_inc(bank_free[3], 1)
                if n == N_XV + 7:
                    for b in range(4):
                        wait_bank(dve, ("xscores", 0), b)
                        link(dve.tensor_reduce(mx[:, 2 * b:2 * b + 2],
                                               X[:, b, :].rearrange("p (h k) -> p h k", h=2), AX.X, ALU.max))
                        dve.tensor_scalar(nmx[:, 2 * b:2 * b + 2], mx[:, 2 * b:2 * b + 2], -X_SCALE, None,
                                          ALU.mult).then_inc(xmax_ready, 1)
                if n == N_XO:
                    for b in range(4):
                        wait_kept(dve, ("xscores", 0), b)
                    link(dve.reciprocal(rsum[:], rsum[:]))
                    for m in range(M):
                        dve.tensor_tensor(xp[:, m, :, :], xp[:, m, :, :],
                                          rsum[:, 4 * m:4 * m + 4].unsqueeze(2).to_broadcast([P, XH, SEQ]),
                                          ALU.mult).then_inc(xp_ready, 1)
                if n == N_XO + 2:
                    for e in range(2):
                        wait_bank(dve, ("xturn_p1", 0), 2 + e)
                        dve.tensor_copy(xpT[:, 1, 2 * e:2 * e + 2, :],
                                        X[:, 2 + e, :].rearrange("p (k t) -> p k t", k=2))\
                           .then_inc(bank_free[2 + e], 1)
                if n == N_XO + 3:
                    for e in range(2):
                        dve.wait_ge(xo_hi, e + 1)
                        dve.tensor_tensor(oT[:, 1, 2 * e:2 * e + 2, :],
                                          X[:, e, :].rearrange("p (k t) -> p k t", k=2),
                                          f32(oT[:, 0, 2 * e:2 * e + 2, :]), ALU.subtract)\
                           .then_inc(bank_free[e], 1)
            for n in range(N_FFN, N_FFN + AHEAD):
                split(n)
                if n == N_FFN + 1:
                    keep_projected(4, BLK_XO + 2, 2, gx)
            keep_projected(4, BLK_XO + 3, 3, gx)
            sum_blocks(4)
            link(factor(4))
            wait_block(dve, BLK_XO + 3)
            for h in range(2):
                add_residual(4, h, xm)
            split_transposed("h3", 3, aT, G_FFN)

            def hidden(pair):
                blk = BLK_FFN + 1
                dve.wait_ge(chunk_used, N_FFN + 2 * CPB + pair * 2 * CPB)
                wait_block(dve, blk - 1, 4 * pair)
                for m in range(M):
                    dve.scalar_tensor_tensor(out=hid[:, m, :], in0=acc[:, 2 * (blk % 2) + m, :],
                                             scalar=rstd[:, 5, m:m + 1], in1=hid[:, m, :], op0=ALU.mult,
                                             op1=ALU.mult).then_inc(acc_free, 1)

            def keep_hidden(i):
                dve.wait_ge(bank_full[1], TURN[("hidden", 0), 1] + 1 + i)
                k_tiles = slice(4 * i + 2, 4 * i + 4) if isinstance(i, int) else bass.ds(i * 4 + 2, 2)
                dve.tensor_copy(hT[:, k_tiles, :], X[:, 1, :].rearrange("p (k t) -> p k t", k=2))\
                   .then_inc(bank_free[1], 1)

            for n in range(N_FFN + AHEAD, N_FFN + 2 * CPB):
                split(n)
                if n == N_FFN + CPB:
                    factor(5).then_inc(norm_ready, 1)
                    wait_norm(dve, 5)
            with dve.Fori(1, FBLOCKS) as i:
                for c in range(2 * CPB):
                    split(N_FFN + c, 2 * CPB, i)
                    if c == 3:
                        hidden(i - 1)
                    if c == CPB + 2:
                        keep_hidden(i - 1)

            def split_hidden(i, k):
                dve.wait_ge(hq_hi, i * DOWN_UNROLL + k + 1)
                kt = bass.ds(i * DOWN_UNROLL + k, 1) if not isinstance(i, int) else slice(k, k + 1)
                dve.tensor_tensor(hq[:, k, 1:2, :], hT[:, kt, :], f32(hq[:, k, 0:1, :]), ALU.subtract)\
                   .then_inc(hq_lo, 1)

            for k in range(DOWN_UNROLL):
                split_hidden(0, k)
            for c in range(2 * DOWN_UNROLL):
                split(N_DOWN + c)
                if c == AHEAD - 1:
                    hidden(FBLOCKS - 1)
                if c == DOWN_UNROLL:
                    keep_hidden(FBLOCKS - 1)
            with dve.Fori(1, DOWN_TURNS) as i:
                for k in range(DOWN_UNROLL):
                    split_hidden(i, k)
                    for c in (2 * k, 2 * k + 1):
                        split(N_DOWN + c, 2 * DOWN_UNROLL, i)
            sum_blocks(6)
            link(factor(6))
            dve.wait_ge(gain_in, 48)
            for m in range(M):
                for j in range(4):
                    src = (acc if j < 2 else X)[:, 2 * (j % 2) + m, :]
                    cols = slice(j * COLS, (j + 1) * COLS)
                    link(dve.scalar_tensor_tensor(out=scaled[:, j % 2, :], in0=src, scalar=rstd[:, 6, m:m + 1],
                                                  in1=gf[:, cols], op0=ALU.mult, op1=ALU.mult))
                    ins = dve.tensor_tensor(xm[:, m, cols], xm[:, m, cols], scaled[:, j % 2, :], ALU.add)
                    if j % 2:
                        ins.then_inc(out_ready, 1)


BIG = ["x", "mem", "positions", "w_in", "w_attn_branch", "w_ssd_branch", "w_out", "xa_wq", "xa_wk", "xa_wv",
       "xa_wo", "ffn_wg", "ffn_wu", "ffn_wd"]


def constants():
    c = np.zeros((P, C_TOTAL), np.float32)
    r = np.arange(P)
    c[:, C_IDENT:C_IDENT + P] = np.eye(P)
    c[:, C_TRI:C_TRI + P] = r[:, None] <= r[None, :]
    chunk = r[:, None] // 64
    key0, key1 = np.arange(P)[None, :] // 64, 1 + np.arange(192)[None, :] // 64
    c[:, C_AM0:C_AM0 + P] = np.where(key0 <= chunk, 0, NEG)
    c[:, C_AM1:C_AM1 + 192] = np.where((key1 <= chunk + 2) & (key1 >= chunk + 1), 0, NEG)
    c[:, C_CNEG:C_CNEG + P] = np.where(r[:, None] <= r[None, :], 0, NEG)
    c[:, C_FREQ:C_FREQ + 32] = np.float32(10000.0) ** (-np.arange(0, HD, 2, dtype=np.float32) / np.float32(HD))
    c[:, C_SEL:C_SEL + HEADS] = r[:, None] % HEADS == np.arange(HEADS)[None, :]
    c[:, C_EPS] = EPS
    return c


def kernel(**inputs):
    import concourse.bacc as bacc
    from concourse.bass_utils import run_bass_kernel_spmd

    nc = bacc.Bacc("TRN2", target_bir_lowering=False, num_devices=1)
    given = {k: np.asarray(v) for k, v in inputs.items()}
    arrays = {}
    for name in BIG:
        a = given[name]
        arrays[name] = np.ascontiguousarray(a if name in ("x", "mem", "positions") else a[0])
    arrays["positions"] = np.ascontiguousarray(given["positions"].reshape(M, P).T)

    def columns(a):
        return np.ascontiguousarray(a.reshape(-1, P).T)

    arrays["params"] = np.concatenate([columns(given[k]) for k in (
        "mix_pre_g", "xa_pre_g", "xa_mem_g", "ffn_pre_g", "ssd_norm_g", "conv_b", "conv_w")], axis=1)
    arrays["rows"] = np.concatenate([given[k] for k in ("dt_bias", "a_log", "d_skip", "attn_sink")], axis=1)
    arrays["post_gains"] = np.concatenate([given[k] for k in ("mix_post_g", "xa_post_g", "ffn_post_g")], axis=0)
    arrays["consts"] = constants()
    args = [nc.dram_tensor(f"in_{k}", a.shape, mybir.dt.from_np(a.dtype), kind="ExternalInput").ap()
            for k, a in arrays.items()]
    out = nc.dram_tensor("out", given["x"].shape, F32, kind="ExternalOutput").ap()
    trunk(nc, *args, out)
    r = run_bass_kernel_spmd(nc, [{f"in_{k}": a for k, a in arrays.items()}], core_ids=[0])
    return r.results[0]["out"]
```

```python
from contextlib import ExitStack

import numpy as np

import concourse.bass as bass
from concourse import mybir

F32 = mybir.dt.float32
FR = mybir.dt.float32r
BF16 = mybir.dt.bfloat16
I32 = mybir.dt.int32
ACT = mybir.ActivationFunctionType
ALU = mybir.AluOpType
AX = mybir.AxisListType

P = 128
SEQ = 256
M = SEQ // P
D = 2048
KT = D // P
COLS = 512
EPS = 1e-6
HD = 64
HEADS = 32
KV = 8
GROUPS = 4
HPG = HEADS // GROUPS
ATT_SCALE = HD ** -0.5
XH = 4
X_SCALE = P ** -0.5
FFN = 5632
FBLOCKS = FFN // COLS
FKT = FFN // P
NEG = -1e30

Q0, K0, V0, Z0 = 0, 2048, 2560, 3072
XS0, B0, C0, DT0, GA0, GS0 = 5120, 7168, 7680, 8192, 8224, 10272

RAW = 8
SPLIT = 4
AHEAD = 4
KPC = 2
CPB = KT // KPC

MIX_ORDER = [("k", 0), ("v", 0), ("q", 0), ("B", 0), ("q", 1), ("C", 0), ("dt", 0), ("q", 2), ("xs", 0),
             ("q", 3), ("z", 0), ("xs", 1), ("z", 1), ("xs", 2), ("z", 2), ("xs", 3), ("z", 3)]
for _j in range(4):
    MIX_ORDER += [("ga", _j), ("att", _j)]
MIX_ORDER += [("gs", 0), ("y", 0)]
START, ACC = {}, {}
_n = _blk = 0
for _b in MIX_ORDER:
    START[_b] = _n
    if _b[0] == "dt":
        _n += 1
        continue
    ACC[_b] = _blk
    _n += CPB
    _blk += 1
N_LOOP_Y, BLK_LOOP_Y = _n, _blk
LOOP_Y = 3
N_OUT, BLK_OUT = _n + LOOP_Y * 2 * CPB, _blk + LOOP_Y * 2
N_XK, BLK_XK = N_OUT + 4 * CPB, BLK_OUT + 4
N_XQ, BLK_XQ = N_XK + CPB, BLK_XK + 1
N_XV, BLK_XV = N_XQ + CPB, BLK_XQ + 1
N_XO, BLK_XO = N_XV + CPB, BLK_XV + 1
N_FFN, BLK_FFN = N_XO + 8, BLK_XO + 4
N_DOWN, BLK_DOWN = N_FFN + FBLOCKS * 2 * CPB, BLK_FFN + 2 * FBLOCKS
DOWN_UNROLL = 4
DOWN_TURNS = FKT // DOWN_UNROLL
N_END = N_DOWN + 2 * FKT


def end_of(b):
    return START[b] + CPB


PE_STEPS, ACT_STEPS, DVE_STEPS = {}, {}, {}


def at(n, arg, pe=(), act=(), dve=()):
    for table, steps in ((PE_STEPS, pe), (ACT_STEPS, act), (DVE_STEPS, dve)):
        for name, behind in steps:
            table.setdefault(n + behind, []).append((name, arg))


at(0, 0, act=[("squares_x", 4), ("convert_consts", 5), ("root_x", 6), ("angles", 7)],
   dve=[("angles", 6), ("norm_x", 7)])
at(end_of(("k", 0)), 0, pe=[("turn_k", 5)], act=[("keep_k", 9)], dve=[("rope_k", 3)])
at(end_of(("v", 0)), 0, act=[("keep_v", 4)])
for _b in range(4):
    _n = end_of(("q", _b))
    at(_n, _b, pe=[("turn_q", 4)], act=[("keep_q", 8)], dve=[("rope_q", 5)])
    for _h in range(2):
        at(_n + 7 * _h, 2 * _b + _h,
           pe=[("scores", 6), ("turn_p", 10), ("pv", 11)],
           act=[("exponents", 10), ("keep_p", 14), ("keep_o", 15)],
           dve=[("maxima", 9), ("probabilities", 11), ("keep_p", 14), ("keep_o", 15)])
at(START[("dt", 0)], 0, pe=[("turn_dt", 0), ("decay_sums", 7)],
   act=[("keep_dt", 4), ("delta_exp", 6), ("keep_sums", 12), ("sums_hi", 14)],
   dve=[("delta_in", 5), ("delta_series", 6), ("delta_out", 8), ("keep_sums", 13), ("sums_lo", 14)])
for _i, _b in enumerate([("B", 0), ("C", 0)] + [("xs", g) for g in range(4)]):
    _n = end_of(_b)
    at(_n, _i, pe=[("turn_u", 2)], dve=[("taps", 6)], act=[("keep_u", 4), ("last_tap", 6), ("silu", 8)])
    if _b[0] == "xs":
        _n += 0 if _b[1] else 2
        at(_n, _b[1], pe=[("turn_xs", 10)], act=[("keep_xs", 14)], dve=[("keep_xs", 14)])
for _g in range(GROUPS):
    _n = end_of(("z", _g))
    at(_n, _g, pe=[("cb", 1)], act=[("keep_z", 6), ("keep_cb", 5)])
    at(_n, 3 * _g, pe=[("seg", 1), ("y_part", 4)], act=[("decay", 5)], dve=[("decay", 6)])
    at(_n, 3 * _g + 1, pe=[("seg", 4)], act=[("decay", 8)], dve=[("decay", 9)])
    at(_n, 2 * _g, act=[("gate_root", 9)], dve=[("gate_y", 9), ("norm_y", 11)])
    _n += 0 if _g else 5
    at(_n, 3 * _g + 1, pe=[("y_part", 7)])
    at(_n, 3 * _g + 2, pe=[("seg", 7), ("y_part", 11)], act=[("decay", 11)], dve=[("decay", 13)])
    at(_n, 2 * _g + 1, act=[("gate_root", 15)], dve=[("gate_y", 15), ("norm_y", 15)])
    at(_n, _g, pe=[("turn_y", 14)], act=[("keep_y", 17)], dve=[("keep_y", 17)])
for _j in range(4):
    at(end_of(("ga", _j)), ("ga", _j), act=[("sigmoid", 3)])
    at(end_of(("att", _j)), _j, dve=[("merge_att", 3)])
at(end_of(("gs", 0)), ("gs", 0), act=[("sigmoid", 3)])
for _table in (PE_STEPS, ACT_STEPS, DVE_STEPS):
    assert max(_table) < N_LOOP_Y

BANKS = {"turn_k": (0, 1, 2, 3), "turn_q": (2, 3), "scores": (0, 1), "turn_p": (0, 1), "pv": (3, 2),
         "turn_dt": (), "decay_sums": (2,), "turn_u": (0, 1), "turn_xs": (0, 1), "cb": (2,), "seg": (0, 1),
         "turn_y": (2, 3)}
TURN = {}
_used = [0] * 4


def use_banks(key, banks):
    for b in banks:
        TURN[key, b] = _used[b]
        _used[b] += 1


X_T = 8
for _j in range(X_T):
    use_banks(("x", _j), (_j % 4,))
for _n in range(N_LOOP_Y):
    if _n == START[("dt", 0)]:
        use_banks(("dt", 0), (3,))
    for _name, _arg in PE_STEPS.get(_n, []):
        if _name == "y_part":
            if _arg % 3 != 2:
                use_banks(("y_bank", 2 * (_arg // 3) + _arg % 3), (3,))
        else:
            use_banks((_name, _arg), BANKS[_name])
for _i in range(LOOP_Y + 1):
    use_banks(("merged", _i), (0, 1))
for _j in range(X_T):
    use_banks(("mem", _j), (_j % 4,))
for _j in range(X_T):
    use_banks(("h2", _j), (_j % 4,))
use_banks(("xk", 0), (0, 1))
use_banks(("xq", 0), (2, 3))
use_banks(("xscores", 0), (0, 1, 2, 3))
use_banks(("xturn_p0", 0), (0, 1))
use_banks(("xturn_p1", 0), (2, 3))
use_banks(("xpv", 0), (0, 1))
for _j in range(X_T):
    use_banks(("h3", _j), (_j % 4,))
for _i in range(FBLOCKS):
    use_banks(("hidden", _i), (0, 1))
use_banks(("down", 0), (0, 1, 2, 3))

CONV_UNITS = [("B", 0), ("C", 0)] + [("xs", g) for g in range(GROUPS)]

G_MIX, G_XA, G_MEM, G_FFN, G_SSD, CONV_B, CONV_W = 0, 16, 32, 48, 64, 80, 104
PARAMS = CONV_W + 96
R_DTB, R_ALOG, R_DSKIP, R_SINK = 0, 32, 64, 96
ROWS = 128
C_IDENT, C_TRI, C_MASK, C_CNEG, C_FREQ, C_SEL, C_EPS, C_TOTAL = 0, 128, 256, 384, 512, 544, 576, 577


def trunk(nc, x, mem, positions, w_in, w_attn_branch, w_ssd_branch, w_out, xa_wq, xa_wk, xa_wv, xa_wo,
          ffn_wg, ffn_wu, ffn_wd, params, rows, post_gains, consts, out):
    ctx = ExitStack()
    with ctx:
        def sem(name):
            return ctx.enter_context(nc.semaphore(name))

        base = 17408
        place = [base]

        def sb(name, shape, dt=F32, offset=None):
            size = int(np.prod(shape[1:])) * (2 if dt == BF16 else 4)
            t = nc.alloc_sbuf_tensor_at(name, shape, dt, offset=place[0] if offset is None else offset)
            if offset is None:
                place[0] += -(-size // 32) * 32
            return t

        KB = 1024
        raw = sb("raw", [P, RAW, KPC * COLS])
        hi = sb("hi", [P, SPLIT, KPC * COLS], FR)
        lo = sb("lo", [P, SPLIT, KPC * COLS], FR)
        at_a = place[0]
        aT = sb("aT", [P, 2, KT, SEQ], FR)
        at_b = place[0]
        bT = sb("bT", [P, 2, KT, SEQ], FR)
        at_c = place[0]
        cT = sb("cT", [P, 2, KT, SEQ], FR)
        at_w = place[0]
        kT = sb("kT", [P, KV, SEQ], offset=at_c)
        vv = sb("vv", [P, 3, KV, 2, HD], offset=at_c + 8 * KB)
        qs = sb("qs", [P, M, COLS], offset=at_c + 20 * KB)
        qT = sb("qT", [P, 4, SEQ], offset=at_c + 24 * KB)
        pT = sb("pT", [P, 2, COLS], offset=at_c + 28 * KB)
        xm = sb("xm", [P, M, D], offset=at_w)
        mix = sb("mix", [P, M, D], offset=at_w + 16 * KB)
        kk = sb("kk", [P, M, KV, 2, HD], offset=at_w)
        bcT = sb("bcT", [P, 2, 4, SEQ], offset=at_w)
        uc = sb("uc", [P, 4 * SEQ], offset=at_w + 8 * KB)
        xs = sb("xs", [P, M, COLS], offset=at_w + 12 * KB)
        xdt = sb("xdt", [P, M, COLS], offset=at_w + 16 * KB)
        lm = sb("lm", [P, HPG, P], offset=at_w + 20 * KB)
        yy = sb("yy", [P, M, COLS], offset=at_w + 24 * KB)
        sz = sb("sz", [P, M, COLS], offset=at_w + 28 * KB)
        place[0] += 32 * KB
        p0 = sb("p0", [P, 4, P])
        p1 = sb("p1", [P, 4, P])
        swapped = sb("swapped", [P, COLS])
        gate = sb("gate", [P, M, COLS], offset=place[0] - 4 * KB)
        csq = sb("csq", [2 * HEADS, 3, P], FR)
        cbs = sb("cbs", [P, 3 * P])
        dt = sb("dt", [P, M, HEADS])
        junk = sb("junk", [P, D], offset=at_c)
        at_t = at_w + 20 * KB
        da2 = sb("da2", [P, M, 2, HEADS], offset=at_t)
        csf = sb("csf", [2 * HEADS, 3, P], offset=at_t + 512)
        chi = sb("chi", [2 * HEADS, 3, P], FR, offset=at_t + 2048)
        sp = sb("sp", [P, 6, M * HEADS], offset=at_t + 3584)
        dtT = sb("dtT", [HEADS, SEQ], offset=at_t + 5120)
        ident = sb("ident", [P, P])
        tri = sb("tri", [P, P])
        mask = sb("mask", [P, P])
        identb = sb("identb", [P, P], BF16)
        cnegb = sb("cnegb", [P, P], BF16)
        sel = sb("sel", [2 * HEADS, 2, HEADS], FR)
        rope = sb("rope", [P, 3, M, 32])
        par = sb("par", [P, PARAMS])
        row = sb("row", [P, ROWS])
        ssq = sb("ssq", [P, 7, M, 4])
        rstd = sb("rstd", [P, 7, M])
        ysq = sb("ysq", [P, M])
        yrs = sb("yrs", [P, M])
        eps = sb("eps", [P, 1])
        mx = sb("mx", [P, 8])
        nmx = sb("nmx", [P, 8])
        esk = sb("esk", [P, 8])
        rsum = sb("rsum", [P, 8])
        assert place[0] <= 229344, place[0]
        ctmp = sb("ctmp", [P, C_TOTAL], offset=at_w + 32 * KB)
        pos = sb("pos", [P, M], I32, offset=at_w + 35 * KB)
        ang = sb("ang", [P, 6, M * 32], offset=at_w + 35 * KB + 64)
        gb = sb("gb", [P, D], offset=at_c + 8 * KB)
        xr = sb("xr", [P, M, D], offset=at_c + 16 * KB)
        gx = sb("gx", [P, D], offset=at_b)
        xqk = sb("xqk", [P, M, COLS], offset=at_b + 8 * KB)
        xqT = sb("xqT", [P, XH, SEQ], offset=at_b + 12 * KB)
        xkT = sb("xkT", [P, XH, SEQ], offset=at_b + 16 * KB)
        xv = sb("xv", [P, M, COLS], offset=at_b + 20 * KB)
        oT = sb("oT", [P, 2, XH, SEQ], FR, offset=at_b + 24 * KB)
        xp = sb("xp", [P, M, XH, SEQ], offset=at_w + 16 * KB)
        xpT = sb("xpT", [P, M, XH, SEQ], offset=at_w + 24 * KB)
        hid = sb("hid", [P, M, COLS], offset=at_w + 16 * KB)
        gf = sb("gf", [P, D], offset=at_w + 20 * KB)
        squared = sb("squared", [P, 4, COLS], offset=at_b)
        projected = sb("projected", [P, M, D], offset=at_b + 8 * KB)
        hT = sb("hT", [P, FKT, SEQ], offset=at_b)
        hq = sb("hq", [P, DOWN_UNROLL, 2, SEQ], FR, offset=at_b + 44 * KB)

        acc = ctx.enter_context(nc.psum_tensor("acc", [P, 4, COLS], F32))
        X = ctx.enter_context(nc.psum_tensor("X", [P, 4, COLS], F32))

        raw_loaded = [sem(f"raw_loaded{s}") for s in range(RAW)]
        hi_ready, lo_ready, chunk_used = sem("hi_ready"), sem("lo_ready"), sem("chunk_used")
        acc_free = sem("acc_free")
        bank_full = [sem(f"bank_full{b}") for b in range(4)]
        bank_free = [sem(f"bank_free{b}") for b in range(4)]
        x_in = [sem(f"x_in{q}") for q in range(4)]
        ident_in, par_in, consts_in, pos_in, mem_in, x_again, gain_in = (
            sem(s) for s in ("ident_in", "par_in", "consts_in", "pos_in", "mem_in", "x_again", "gain_in"))
        out_stored = sem("out_stored")
        load_turn = sem("load_turn")
        act_step, dve_step = sem("act_step"), sem("dve_step")
        consts_ready = sem("consts_ready")
        angles_ready, rope_ready = sem("angles_ready"), sem("rope_ready")
        sum_ready, root_ready, norm_ready = (sem(s) for s in ("sum_ready", "root_ready", "norm_ready"))
        block_sq = sem("block_sq")
        t_hi = sem("t_hi")
        k_roped, q_roped = sem("k_roped"), sem("q_roped")
        max_ready, probs_ready = sem("max_ready"), sem("probs_ready")
        even_scores, o_hi = sem("even_scores"), sem("o_hi")
        tap_ready, silu_ready, xs_ready = (sem(s) for s in ("tap_ready", "silu_ready", "xs_ready"))
        sp_in, sp_exp, da_ready = (sem(s) for s in ("sp_in", "sp_exp", "da_ready"))
        dt_kept, cse_ready, chi_ready, csq_lo = (
            sem(s) for s in ("dt_kept", "cse_ready", "chi_ready", "csq_lo"))
        m_ready, y_done = sem("m_ready"), sem("y_done")
        y_gated, y_root, y_normed = (sem(s) for s in ("y_gated", "y_root", "y_normed"))
        yT_hi = sem("yT_hi")
        merged_ready, merged_hi = sem("merged_ready"), sem("merged_hi")
        resid_ready = sem("resid_ready")
        xmax_ready, xp_ready, xo_hi = (sem(s) for s in ("xmax_ready", "xp_ready", "xo_hi"))
        hq_hi, hq_lo = sem("hq_hi"), sem("hq_lo")
        down_done, out_ready = sem("down_done"), sem("out_ready")

        def wait_bank(eng, key, b):
            eng.wait_ge(bank_full[b], TURN[key, b] + 1)

        def take_bank(pe, key, b):
            if TURN[key, b]:
                pe.wait_ge(bank_free[b], TURN[key, b])

        def wait_kept(eng, key, b, more=0):
            eng.wait_ge(bank_free[b], TURN[key, b] + 1 + more)

        def wait_norm(eng, norm):
            eng.wait_ge(norm_ready, {0: 1, 1: 2, 3: 3, 5: 4}[norm])

        def wait_block(eng, blk, more=0):
            eng.wait_ge(acc_free, 2 * (blk + 1) + more)

        block = ctx.enter_context(nc.Block())

        @block.sync
        def _(sp_):
            def load(n, turns, i, dst, src):
                slot, count = n % RAW, n // RAW + 1
                if n >= RAW:
                    sp_.wait_ge(lo_ready, n - RAW + 1 + turns * i)
                if turns:
                    sp_.sem_inc(load_turn, 1)
                sp_.dma_start(dst(raw[:, slot, :]), src).then_inc(raw_loaded[slot], 16)

            def load_block(n, turns, i, w, col, k_tiles=KT):
                rows_ = w.rearrange("(t p) n -> p t n", p=P)
                for c in range(k_tiles // KPC):
                    load(n + c, turns, i, lambda s: s.rearrange("p (k n) -> p k n", k=KPC),
                         rows_[:, c * KPC:(c + 1) * KPC, col])

            sp_.dma_start(ident[:], consts[:, C_IDENT:C_IDENT + P]).then_inc(ident_in, 16)
            for q in range(4):
                cols = slice(q * COLS, (q + 1) * COLS)
                sp_.dma_start(xm[:, :, cols], x[:, :, cols].rearrange("b (m p) d -> p (b m) d", p=P))\
                   .then_inc(x_in[q], 16)
            sp_.dma_start(par[:], params).then_inc(par_in, 16)
            columns = {"q": Q0, "k": K0, "v": V0, "z": Z0, "xs": XS0, "B": B0, "C": C0, "ga": GA0, "gs": GS0}
            for b in MIX_ORDER:
                kind, j = b
                if kind == "dt":
                    load(START[b], 0, 0, lambda s: s[:, 0:KT * HEADS].rearrange("p (k n) -> p k n", k=KT),
                         w_in[:, DT0:DT0 + HEADS].rearrange("(t p) n -> p t n", p=P))
                    continue
                w = {"att": w_attn_branch, "y": w_ssd_branch}.get(kind, w_in)
                c0 = columns.get(kind, 0) + j * COLS
                load_block(START[b], 0, 0, w, slice(c0, c0 + COLS))
                if b == ("k", 0):
                    sp_.dma_start(pos[:], positions).then_inc(pos_in, 16)
                    for t, c0 in ((ctmp, 0), (tri, C_TRI), (mask, C_MASK)):
                        sp_.dma_start(t[:], consts[:, c0:c0 + t.shape[1]]).then_inc(consts_in, 16)
                    sp_.dma_start(row[:], rows.to_broadcast([P, ROWS])).then_inc(consts_in, 16)
            with sp_.Fori(0, LOOP_Y) as i:
                load_block(N_LOOP_Y, 2 * CPB, i, w_in, bass.ds((i + 1) * COLS + GS0, COLS))
                load_block(N_LOOP_Y + CPB, 2 * CPB, i, w_ssd_branch, bass.ds((i + 1) * COLS, COLS))
            for j in range(4):
                load_block(N_OUT + j * CPB, 0, 0, w_out, slice(j * COLS, (j + 1) * COLS))
                if j == 0:
                    sp_.wait_ge(chunk_used, N_OUT)
                    sp_.dma_start(gb[:], post_gains[0:1, :].to_broadcast([P, D])).then_inc(gain_in, 16)
                if j == 1:
                    sp_.wait_ge(merged_ready, LOOP_Y + 1)
                    sp_.dma_start(xm[:], mem.rearrange("b (m p) d -> p (b m) d", p=P)).then_inc(mem_in, 16)
                if j == 2:
                    sp_.dma_start(xr[:], x.rearrange("b (m p) d -> p (b m) d", p=P)).then_inc(x_again, 16)
            load_block(N_XK, 0, 0, xa_wk, slice(0, COLS))
            sp_.wait_ge(chunk_used, N_XK)
            sp_.dma_start(gx[:], post_gains[1:2, :].to_broadcast([P, D])).then_inc(gain_in, 16)
            load_block(N_XQ, 0, 0, xa_wq, slice(0, COLS))
            load_block(N_XV, 0, 0, xa_wv, slice(0, COLS))
            for j in range(4):
                load_block(N_XO + 2 * j, 0, 0, xa_wo, slice(j * COLS, (j + 1) * COLS), k_tiles=XH)
            with sp_.Fori(0, FBLOCKS) as i:
                load_block(N_FFN, 2 * CPB, i, ffn_wg, bass.ds(i * COLS, COLS))
                load_block(N_FFN + CPB, 2 * CPB, i, ffn_wu, bass.ds(i * COLS, COLS))
            sp_.wait_ge(root_ready, 6)
            sp_.dma_start(gf[:], post_gains[2:3, :].to_broadcast([P, D])).then_inc(gain_in, 16)
            for c in range(2 * DOWN_UNROLL):
                k, half = c % DOWN_UNROLL, c // DOWN_UNROLL
                load(N_DOWN + c, 0, 0, lambda s: s, ffn_wd[k * P:(k + 1) * P, half * 1024:(half + 1) * 1024])
            with sp_.Fori(1, DOWN_TURNS) as i:
                for c in range(2 * DOWN_UNROLL):
                    half = c % 2
                    load(N_DOWN + c, 2 * DOWN_UNROLL, i, lambda s: s,
                         ffn_wd[bass.ds((i * DOWN_UNROLL + c // 2) * P, P), half * 1024:(half + 1) * 1024])
            for q in range(4 * M):
                m, cols = q // 4, slice(q % 4 * COLS, (q % 4 + 1) * COLS)
                sp_.wait_ge(out_ready, q + 1)
                sp_.dma_start(out[0, m * P:(m + 1) * P, cols], xm[:, m, cols]).then_inc(out_stored, 16)
            sp_.wait_ge(out_stored, 16 * 4 * M)

        @block.tensor
        def _(pe):
            def step(name, arg):
                PE[name](arg)

            def block_products(n, blk, lhs, turns=0, blk_turns=0, i=0, k_tiles=KT, steps=True, ready=None,
                               between=None):
                if blk >= 2:
                    pe.wait_ge(acc_free, 2 * (blk - 1) + 2 * blk_turns * i)
                for c in range(k_tiles // KPC):
                    if ready:
                        ready(c)
                    pe.wait_ge(lo_ready, n + c + 1 + turns * i)
                    s = (n + c) % SPLIT
                    for k in range(KPC):
                        kt = c * KPC + k
                        for m in range(M):
                            o = acc[:, 2 * (blk % 2) + m, :]
                            for a, w in ((0, hi), (1, hi), (0, lo)):
                                last = pe.matmul(o, lhs[:, a, kt, m * P:(m + 1) * P],
                                                 w[:, s, k * COLS:(k + 1) * COLS],
                                                 start=(kt == 0 and a == 0 and w is hi),
                                                 stop=(kt == k_tiles - 1 and w is lo))
                    last.then_inc(chunk_used, 1)
                    if steps:
                        for name, arg in PE_STEPS.get(n + c, []):
                            step(name, arg)
                    if between:
                        between(c)

            def transposed(key, b, parts):
                take_bank(pe, key, b)
                for e, piece in enumerate(parts):
                    last = pe.transpose(X[:, b, e * P:(e + 1) * P], piece, ident[:])
                last.then_inc(bank_full[b], 1)

            def rows_transposed(name, src, turns=range(X_T)):
                for j in turns:
                    transposed((name, j), j % 4, [src[:, m, (2 * j + k) * P:(2 * j + k + 1) * P]
                                                  for k in range(2) for m in range(M)])

            def turn_k(_):
                pe.wait_ge(k_roped, 1)
                for b in range(4):
                    transposed(("turn_k", 0), b, [kk[:, m, 2 * b + g, :, :].rearrange("p e d -> p (e d)")
                                                  for g in range(2) for m in range(M)])

            def turn_q(b):
                pe.wait_ge(q_roped, b + 1)
                for e, bank in enumerate(BANKS["turn_q"]):
                    transposed(("turn_q", b), bank, [qs[:, m, (2 * e + t) * P:(2 * e + t + 1) * P]
                                                      for t in range(2) for m in range(M)])

            def scores(u):
                for b in BANKS["turn_q"]:
                    wait_kept(pe, ("turn_q", u // 2), b)
                for b in range(4):
                    wait_kept(pe, ("turn_k", 0), b)
                for b in range(2):
                    take_bank(pe, ("scores", u), b)
                for odd in range(2):
                    r = slice(HD * odd, HD * odd + HD)
                    if odd:
                        pe.wait_ge(even_scores, u + 1)
                    for h in (odd, odd + 2):
                        q = qT[r, 2 * (u % 2) + h // 2, :]
                        last = pe.matmul(X[:, 0, h * P:(h + 1) * P], q[:, 0:P], kT[r, u, 0:P], start=True, stop=True)
                    if odd:
                        last.then_inc(bank_full[0], 1)
                    for h in (odd, odd + 2):
                        q = qT[r, 2 * (u % 2) + h // 2, :]
                        for c in (2, 3):
                            last = pe.matmul(X[(c - 2) * 64:(c - 1) * 64, 1, h * P:(h + 1) * P],
                                             q[:, c * 64:(c + 1) * 64], kT[r, u, (c - 1) * 64:(c + 1) * 64],
                                             start=True, stop=True)
                    last.then_inc(bank_full[1] if odd else even_scores, 1)

            def turn_p(u):
                pe.wait_ge(probs_ready, u + 1)
                transposed(("turn_p", u), 0, [p0[:, h, :] for h in range(4)])
                transposed(("turn_p", u), 1, [p1[:, h, :] for h in range(4)])

            def pv(u):
                for b in range(2):
                    wait_kept(pe, ("turn_p", u), b)
                wait_block(pe, ACC[("v", 0)])
                v = [vv[:, t, u, :, :].rearrange("p e d -> p (e d)") for t in range(3)]
                b0, b1 = BANKS["pv"]
                take_bank(pe, ("pv", u), b0)
                pe.matmul(X[:, b0, :], v[0], pT[:, 0, :], start=True, stop=True).then_inc(bank_full[b0], 1)
                take_bank(pe, ("pv", u), b1)
                for c, t in ((2, 2), (3, 1)):
                    of_chunk = slice((c - 2) * 64, (c - 1) * 64)
                    last = pe.matmul(X[:, b1, :].rearrange("p (h t) -> p h t", h=4)[:, :, of_chunk], v[t],
                                     pT[:, 1, :].rearrange("p (h t) -> p h t", h=4)[:, :, of_chunk],
                                     start=True, stop=True)
                last.then_inc(bank_full[b1], 1)

            def dt_products():
                n = START[("dt", 0)]
                pe.wait_ge(lo_ready, n + 1)
                take_bank(pe, ("dt", 0), 3)
                s = n % SPLIT
                for kt in range(KT):
                    for a, w in ((0, hi), (1, hi), (0, lo)):
                        last = pe.matmul(X[0:HEADS, 3, 0:SEQ], w[:, s, kt * HEADS:(kt + 1) * HEADS], aT[:, a, kt, :],
                                         start=(kt == 0 and a == 0 and w is hi), stop=(kt == KT - 1 and w is lo))
                last.then_inc(chunk_used, 1)

            def turn_dt(_):
                pe.wait_ge(dt_kept, 1)
                for m in range(M):
                    last = pe.transpose(X[:, 3, m * HEADS:(m + 1) * HEADS], dtT[:, m * P:(m + 1) * P],
                                        ident[0:HEADS, 0:HEADS])
                last.then_inc(bank_full[3], 1)

            def decay_sums(_):
                pe.wait_ge(da_ready, 1)
                take_bank(pe, ("decay_sums", 0), 2)
                for m in range(M):
                    last = pe.matmul(X[0:2 * HEADS, 2, m * P:(m + 1) * P],
                                     da2[:, m, :, :].rearrange("p e h -> p (e h)"), tri[:], start=True, stop=True)
                last.then_inc(bank_full[2], 1)

            def turn_u(i):
                wait_block(pe, ACC[CONV_UNITS[i]])
                u3 = uc[:].rearrange("p (m n) -> p m n", m=M)
                for e, bank in enumerate(BANKS["turn_u"]):
                    transposed(("turn_u", i), bank, [u3[:, m, (2 * e + t) * P:(2 * e + t + 1) * P]
                                                  for t in range(2) for m in range(M)])

            def turn_xs(g):
                pe.wait_ge(silu_ready, 3 + g)
                for m, bank in enumerate(BANKS["turn_xs"]):
                    transposed(("turn_xs", g), bank, [uc[:, c * SEQ + m * P:c * SEQ + (m + 1) * P] for c in range(4)])

            def cb(g):
                pe.wait_ge(silu_ready, 2)
                take_bank(pe, ("cb", g), 2)
                pe.matmul(X[:, 2, 0:SEQ], bcT[:, 0, g, 0:P], bcT[:, 1, g, :], start=True, stop=True)
                pe.matmul(X[:, 2, SEQ:SEQ + P], bcT[:, 0, g, P:SEQ], bcT[:, 1, g, P:SEQ], start=True,
                          stop=True).then_inc(bank_full[2], 1)

            def add_nothing(b, start):
                return pe.matmul(X[:, b, :].rearrange("p (h l) -> p h l", h=4), identb[0:1, :],
                                 cnegb[0:1, :].unsqueeze(1).to_broadcast([1, 4, P]), start=start, stop=not start)

            def seg(i):
                g, part = i // 3, i % 3
                l_of, s_of, masked = ((0, 0, True), (1, 2, False), (1, 1, True))[part]
                pe.wait_ge(chi_ready, 1)
                pe.wait_ge(csq_lo, 1)
                pe.wait_ge(consts_ready, 1)
                for b in range(2):
                    take_bank(pe, ("seg", i), b)
                    h0 = HPG * g + 4 * b
                    o3 = X[:, b, :].rearrange("p (h l) -> p h l", h=4)
                    pe.matmul(o3, csq[:, s_of, :], sel[:, 1, h0:h0 + 4].unsqueeze(2).to_broadcast([2 * HEADS, 4, P]),
                              start=True, stop=False)
                    for h in range(4):
                        pe.matmul(X[:, b, h * P:(h + 1) * P], sel[:, 0, h0 + h:h0 + h + 1].to_broadcast([2 * HEADS, P]),
                                  csq[:, l_of, :], start=False, stop=False, skip_group_check=True)
                    if masked:
                        last = pe.matmul(o3, identb[:], cnegb[:].unsqueeze(1).to_broadcast([P, 4, P]),
                                         start=False, stop=True)
                    else:
                        last = add_nothing(b, start=False)
                    last.then_inc(bank_full[b], 1)

            def y_part(i):
                g, part = i // 3, i % 3
                pe.wait_ge(m_ready, i + 1)
                for b in BANKS["turn_xs"]:
                    wait_kept(pe, ("turn_xs", g), b)
                if part < 2:
                    take_bank(pe, ("y_bank", 2 * g + part), 3)
                src = (0, 0, 1)[part]
                if part == 1:
                    add_nothing(3, start=True)
                for h in range(HPG):
                    last = pe.matmul(X[:, 3, h * HD:(h + 1) * HD], lm[:, h, :], xdt[:, src, h * HD:(h + 1) * HD],
                                     start=(part == 0), stop=(part == 0), skip_group_check=True)
                if part == 2:
                    last = add_nothing(3, start=False)
                last.then_inc(y_done if part == 1 else bank_full[3], 1)

            def turn_y(g):
                pe.wait_ge(y_normed, M * (g + 1))
                for e in range(2):
                    transposed(("turn_y", g), 2 + e, [yy[:, m, (2 * e + t) * P:(2 * e + t + 1) * P]
                                                      for t in range(2) for m in range(M)])

            PE = dict(turn_dt=turn_dt, turn_k=turn_k, turn_q=turn_q, scores=scores, turn_p=turn_p, pv=pv,
                      decay_sums=decay_sums, turn_u=turn_u, turn_xs=turn_xs, cb=cb, seg=seg, y_part=y_part,
                      turn_y=turn_y)

            pe.wait_ge(ident_in, 16)
            for q in range(4):
                pe.wait_ge(x_in[q], 16)
                rows_transposed("x", xm, range(2 * q, 2 * q + 2))

            def split_of(name):
                return lambda c: wait_kept(pe, (name, c), c % 4)

            for b in MIX_ORDER:
                kind, j = b
                n = START[b]
                if kind == "dt":
                    dt_products()
                    for name, arg in PE_STEPS.get(n, []):
                        step(name, arg)
                    continue
                if b == ("k", 0):
                    block_products(n, ACC[b], aT, ready=split_of("x"))
                elif kind == "att":
                    if j == 0:
                        for bank in BANKS["pv"]:
                            wait_kept(pe, ("pv", KV - 1), bank)
                    block_products(n, ACC[b], bT)
                elif kind == "y":
                    wait_kept(pe, ("turn_y", GROUPS - 1), 2)
                    wait_kept(pe, ("turn_y", GROUPS - 1), 3)
                    block_products(n, ACC[b], cT)
                else:
                    block_products(n, ACC[b], aT)

            def turn_fresh(turn):
                pe.wait_ge(merged_ready, turn)
                for e in range(2):
                    for q in range(4):
                        last = pe.transpose(X[:, e, q * P:(q + 1) * P],
                                            yy[:, q % 2, (2 * e + q // 2) * P:(2 * e + q // 2 + 1) * P], ident[:])
                    last.then_inc(bank_full[e], 1)

            with pe.Fori(0, LOOP_Y) as i:
                def fresh(c):
                    if c == 5:
                        for e in range(2):
                            pe.wait_ge(bank_free[e], i + TURN[("merged", 0), e])
                        turn_fresh(i + 1)
                block_products(N_LOOP_Y, BLK_LOOP_Y, aT, 2 * CPB, 2, i, steps=False, between=fresh)
                block_products(N_LOOP_Y + CPB, BLK_LOOP_Y + 1, cT, 2 * CPB, 2, i, steps=False)

            def out_ready_(c):
                if c == 0:
                    wait_kept(pe, ("merged", LOOP_Y - 1), 0)
                    wait_kept(pe, ("merged", LOOP_Y - 1), 1)
                if c == 6:
                    wait_kept(pe, ("merged", LOOP_Y), 0)
                    wait_kept(pe, ("merged", LOOP_Y), 1)

            def last_merged(c):
                if c == 3:
                    for e in range(2):
                        take_bank(pe, ("merged", LOOP_Y), e)
                    turn_fresh(LOOP_Y + 1)

            def beside_last(c):
                if c in (0, 3):
                    pe.wait_ge(mem_in, 16)
                    rows_transposed("mem", xm, range(4) if c == 0 else range(4, X_T))

            for j in range(4):
                block_products(N_OUT + j * CPB, BLK_OUT + j, bT, steps=False,
                               ready=out_ready_ if j == 0 else None,
                               between={0: last_merged, 3: beside_last}.get(j))

            def turn_heads(key, blk, first_bank):
                wait_block(pe, blk)
                for e in range(2):
                    transposed((key, 0), first_bank + e, [xqk[:, m, (2 * e + t) * P:(2 * e + t + 1) * P]
                                                          for t in range(2) for m in range(M)])

            def xscores():
                for b in range(2):
                    wait_kept(pe, ("xk", 0), b)
                    wait_kept(pe, ("xq", 0), 2 + b)
                for b in range(4):
                    take_bank(pe, ("xscores", 0), b)
                    m = b // 2
                    for h in range(2 * (b % 2), 2 * (b % 2) + 2):
                        last = pe.matmul(X[:, b, (h % 2) * SEQ:(h % 2 + 1) * SEQ], xqT[:, h, m * P:(m + 1) * P],
                                         xkT[:, h, :], start=True, stop=True)
                    last.then_inc(bank_full[b], 1)

            def turn_xp():
                pe.wait_ge(xp_ready, M)
                for t in range(M):
                    for e in range(2):
                        transposed((f"xturn_p{t}", 0), 2 * t + e,
                                   [xp[:, m, 2 * e + h, t * P:(t + 1) * P] for h in range(2) for m in range(M)])

            def beside_xk(c):
                if c in (4, 6):
                    pe.wait_ge(resid_ready, c - 2)
                    rows_transposed("h2", xm, range(4) if c == 4 else range(4, X_T))

            def beside_xq(c):
                if c == 2:
                    turn_heads("xk", BLK_XK, 0)

            def beside_xv(c):
                if c == 1:
                    turn_heads("xq", BLK_XQ, 2)
                if c == 3:
                    xscores()
                if c == 6:
                    turn_xp()

            block_products(N_XK, BLK_XK, aT, steps=False, ready=split_of("mem"), between=beside_xk)
            block_products(N_XQ, BLK_XQ, cT, steps=False, ready=split_of("h2"), between=beside_xq)
            block_products(N_XV, BLK_XV, aT, steps=False, between=beside_xv)
            for b in range(4):
                wait_kept(pe, (f"xturn_p{b // 2}", 0), b)
            wait_block(pe, BLK_XV)
            for e in range(2):
                take_bank(pe, ("xpv", 0), e)
                for h in range(2 * e, 2 * e + 2):
                    for t in range(M):
                        last = pe.matmul(X[:, e, (h % 2) * SEQ:(h % 2 + 1) * SEQ], xv[:, t, h * P:(h + 1) * P],
                                         xpT[:, t, h, :], start=(t == 0), stop=(t == 1))
                last.then_inc(bank_full[e], 1)
            for j in range(4):
                block_products(N_XO + 2 * j, BLK_XO + j, oT, k_tiles=XH, steps=False,
                               ready=(lambda c: wait_kept(pe, ("xpv", 0), c)) if j == 0 else None)
            for h in range(2):
                pe.wait_ge(resid_ready, 5 + h)
                rows_transposed("h3", xm, range(2 * h, 2 * h + 2))

            def beside_first(c):
                if c in (0, 1):
                    pe.wait_ge(resid_ready, 7 + c)
                    rows_transposed("h3", xm, range(4 + 2 * c, 6 + 2 * c))

            def turn_hidden(i):
                pe.wait_ge(acc_free, i * 4 + 2 * BLK_FFN)
                for e in range(2):
                    pe.wait_ge(bank_free[e], i - 1 + TURN[("hidden", 0), e])
                    for q in range(4):
                        last = pe.transpose(X[:, e, q * P:(q + 1) * P],
                                            hid[:, q % 2, (2 * e + q // 2) * P:(2 * e + q // 2 + 1) * P], ident[:])
                    last.then_inc(bank_full[e], 1)

            block_products(N_FFN, BLK_FFN, aT, steps=False, ready=split_of("h3"), between=beside_first)
            block_products(N_FFN + CPB, BLK_FFN + 1, aT, steps=False)
            with pe.Fori(1, FBLOCKS) as i:
                block_products(N_FFN, BLK_FFN, aT, 2 * CPB, 2, i, steps=False,
                               between=lambda c: turn_hidden(i) if c == 6 else None)
                block_products(N_FFN + CPB, BLK_FFN + 1, aT, 2 * CPB, 2, i, steps=False)

            def down(c, i, k, half, start, stop):
                pe.wait_ge(hq_lo, i * DOWN_UNROLL + k + 1)
                pe.wait_ge(lo_ready, N_DOWN + c + 1 + 2 * DOWN_UNROLL * i)
                s = (N_DOWN + c) % SPLIT
                banks = acc if half == 0 else X
                for j in (BLK_DOWN % 2, 1 - BLK_DOWN % 2):
                    if start and c == 0:
                        pe.wait_ge(acc_free, 2 * (BLK_DOWN - 1 if j == BLK_DOWN % 2 else BLK_DOWN))
                    for m in range(M):
                        for a, w in ((0, hi), (1, hi), (0, lo)):
                            last = pe.matmul(banks[:, 2 * j + m, :], hq[:, k, a, m * P:(m + 1) * P],
                                             w[:, s, j * COLS:(j + 1) * COLS],
                                             start=(start and a == 0 and w is hi), stop=(stop and w is lo),
                                             skip_group_check=True)
                        if stop:
                            last.then_inc(down_done, 1)
                if not stop:
                    last.then_inc(chunk_used, 1)

            for c in range(2 * DOWN_UNROLL):
                if c == 1:
                    turn_hidden(FBLOCKS)
                if c == DOWN_UNROLL:
                    for b in range(4):
                        take_bank(pe, ("down", 0), b)
                down(c, 0, c % DOWN_UNROLL, c // DOWN_UNROLL, c % DOWN_UNROLL == 0, False)
            with pe.Fori(1, DOWN_TURNS - 1) as i:
                for c in range(2 * DOWN_UNROLL):
                    down(c, i, c // 2, c % 2, False, False)
            for c in range(2 * DOWN_UNROLL):
                down(c, DOWN_TURNS - 1, c // 2, c % 2, False, c // 2 == DOWN_UNROLL - 1)

        @block.scalar
        def _(act):
            own = [0]

            def link(ins):
                own[0] += 1
                ins.then_inc(act_step, 1)
                act.wait_ge(act_step, own[0])

            def split(n, turns=0, i=0, size=KPC * COLS):
                slot = n % RAW
                act.wait_ge(raw_loaded[slot], 16 * (n // RAW + 1) + 16 * (turns // RAW) * i)
                if n >= SPLIT:
                    act.wait_ge(chunk_used, n - SPLIT + 1 + turns * i)
                act.activation(hi[:, n % SPLIT, 0:size], raw[:, slot, 0:size], ACT.Copy).then_inc(hi_ready, 1)

            def split_transposed(name, dst, gain, turns=range(X_T)):
                for j in turns:
                    b = j % 4
                    wait_bank(act, (name, j), b)
                    for k in range(2):
                        kt = 2 * j + k
                        ins = act.activation(dst[:, 0, kt, :], X[:, b, k * SEQ:(k + 1) * SEQ], ACT.Copy,
                                             scale=par[:, gain + kt:gain + kt + 1])
                    ins.then_inc(t_hi, 1)

            def squares(norm, src, m, scratch):
                link(act.activation(scratch, src, ACT.Square, accum_out=ssq[:, norm, m, 0:1]))

            def root(norm):
                if norm in (2, 4, 6):
                    act.wait_ge(sum_ready, norm // 2)
                    src = rstd[:, norm, :]
                else:
                    src = ssq[:, norm, :, 0]
                act.activation(rstd[:, norm, :], src, ACT.Sqrt, bias=eps[:], scale=1.0 / D).then_inc(root_ready, 1)

            def convert_consts(_):
                act.wait_ge(consts_in, 64)
                act.activation(identb[:], ctmp[:, C_IDENT:C_IDENT + P], ACT.Copy)
                act.activation(cnegb[:], ctmp[:, C_CNEG:C_CNEG + P], ACT.Copy)
                for e in range(2):
                    act.activation(sel[:, e, :], ctmp[0:2 * HEADS, C_SEL:C_SEL + HEADS], ACT.Copy, scale=1.0 - 2 * e)
                act.activation(eps[:], ctmp[:, C_EPS:C_EPS + 1], ACT.Copy).then_inc(consts_ready, 1)
                act.wait_ge(consts_ready, 1)

            def squares_x(_):
                for q in range(4):
                    act.wait_ge(x_in[q], 16)
                for m in range(M):
                    squares(0, xm[:, m, :], m, mix[:, m, :])

            def root_x(_):
                root(0)

            def angles(_):
                act.wait_ge(angles_ready, 1)
                act.activation(rope[:, 0:2, :, :].rearrange("p a m f -> p (a m f)"),
                               ang[:, 4:6, :].rearrange("p a f -> p (a f)"), ACT.Sin).then_inc(rope_ready, 1)

            def keep(key, b, dst, k=2):
                wait_bank(act, key, b)
                act.activation(dst, X[:, b, :].rearrange("p (k t) -> p k t", k=k), ACT.Copy)\
                   .then_inc(bank_free[b], 1)

            def keep_k(_):
                for b in range(4):
                    keep(("turn_k", 0), b, kT[:, 2 * b:2 * b + 2, :])

            def keep_v(_):
                wait_norm(act, 0)
                act.wait_ge(chunk_used, end_of(("v", 0)))
                for m in range(M):
                    bank = 2 * (ACC[("v", 0)] % 2) + m
                    of_window = slice(64, P) if m == 0 else slice(0, 64)
                    for t, dst, src in ((m, slice(0, P), slice(0, P)), (2, slice(m * 64, m * 64 + 64), of_window)):
                        for e in range(2):
                            last = act.activation(vv[dst, t, :, e, :],
                                                  acc[src, bank, :].rearrange("p (g d) -> p g d", g=KV), ACT.Copy,
                                                  scale=rstd[src, 0, m:m + 1])
                    last.then_inc(acc_free, 1)

            def keep_q(b):
                for e, bank in enumerate(BANKS["turn_q"]):
                    keep(("turn_q", b), bank, qT[:, 2 * e:2 * e + 2, :])

            def exponents(u):
                act.wait_ge(max_ready, u + 1)
                act.activation(esk[:], esk[:], ACT.Exp)
                for h in range(4):
                    act.activation(p0[:, h, :], p0[:, h, :], ACT.Exp, bias=nmx[:, h:h + 1], scale=ATT_SCALE,
                                   accum_out=rsum[:, h:h + 1])
                for h in range(4):
                    ins = act.activation(p1[:, h, :], X[:, 1, h * P:(h + 1) * P], ACT.Exp, bias=nmx[:, 4 + h:5 + h],
                                         scale=ATT_SCALE, accum_out=rsum[:, 4 + h:5 + h])
                ins.then_inc(bank_free[1], 1)

            def keep_p(u):
                keep(("turn_p", u), 0, pT[:, 0, :].unsqueeze(1), k=1)

            def keep_o(u):
                for m, b in enumerate(BANKS["pv"]):
                    wait_bank(act, ("pv", u), b)
                    o = X[:, b, :].rearrange("p (a e t) -> p a e t", a=2, e=2)
                    for e in range(2):
                        r = slice(HD * e, HD * e + HD)
                        act.activation(bT[r, 0, 2 * u:2 * u + 2, m * P:(m + 1) * P], o[r, :, e, :], ACT.Copy)\
                           .then_inc(o_hi, 1)

            def keep_dt(_):
                act.wait_ge(chunk_used, START[("dt", 0)] + 1)
                act.activation(dtT[:], X[0:HEADS, 3, 0:SEQ], ACT.Copy).then_inc(dt_kept, 1)

            def delta_exp(_):
                act.wait_ge(sp_in, 1)
                act.activation(row[:, R_ALOG:R_ALOG + HEADS], row[:, R_ALOG:R_ALOG + HEADS], ACT.Exp)
                act.activation(sp[:, 2, :], sp[:, 1, :], ACT.Exp, scale=-1.0).then_inc(sp_exp, 1)

            def keep_sums(_):
                wait_bank(act, ("decay_sums", 0), 2)
                act.activation(csf[:, 0:2, :], X[0:2 * HEADS, 2, 0:SEQ].rearrange("p (m l) -> p m l", m=M),
                               ACT.Copy).then_inc(bank_free[2], 1)

            def sums_hi(_):
                act.wait_ge(cse_ready, 1)
                act.activation(chi[:], csf[:], ACT.Copy)
                act.activation(csq[0:HEADS, :, :], csf[0:HEADS, :, :], ACT.Copy).then_inc(chi_ready, 1)

            def keep_u(i):
                b = CONV_UNITS[i]
                act.wait_ge(chunk_used, end_of(b))
                for m in range(M):
                    act.activation(uc[:, m * COLS:(m + 1) * COLS], acc[:, 2 * (ACC[b] % 2) + m, :], ACT.Copy,
                                   scale=rstd[:, 0, m:m + 1]).then_inc(acc_free, 1)

            def last_tap(i):
                t0 = 16 + 4 * i if i < 2 else 4 * (i - 2)
                banks = BANKS["turn_u"]
                for bank in banks:
                    wait_bank(act, ("turn_u", i), bank)
                for c in range(4):
                    act.activation(uc[:, c * SEQ:(c + 1) * SEQ], X[:, banks[c // 2], (c % 2) * SEQ:(c % 2 + 1) * SEQ],
                                   ACT.Identity, bias=par[:, CONV_B + t0 + c:CONV_B + t0 + c + 1],
                                   scale=par[:, CONV_W + 72 + t0 + c:CONV_W + 73 + t0 + c]).then_inc(tap_ready, 1)

            def silu(i):
                for bank in BANKS["turn_u"]:
                    wait_kept(act, ("turn_u", i), bank)
                dst = uc[:] if i >= 2 else bcT[:, i, :, :].rearrange("p g t -> p (g t)")
                act.activation(dst, uc[:], ACT.Silu).then_inc(silu_ready, 1)

            def keep_xs(g):
                for m, bank in enumerate(BANKS["turn_xs"]):
                    wait_bank(act, ("turn_xs", g), bank)
                    act.activation(xs[:, m, :], X[:, bank, :], ACT.Copy).then_inc(xs_ready, 1)

            def keep_z(g):
                act.wait_ge(chunk_used, end_of(("z", g)))
                for m in range(M):
                    act.activation(sz[:, m, :], acc[:, 2 * (ACC[("z", g)] % 2) + m, :], ACT.Silu,
                                   scale=rstd[:, 0, m:m + 1]).then_inc(acc_free, 1)

            def keep_cb(g):
                wait_bank(act, ("cb", g), 2)
                act.activation(cbs[:], X[:, 2, 0:3 * P], ACT.Copy).then_inc(bank_free[2], 1)

            def decay(i):
                for b in range(2):
                    wait_bank(act, ("seg", i), b)
                if i:
                    g, part = (i - 1) // 3, (i - 1) % 3
                    if part == 1:
                        act.wait_ge(y_done, g + 1)
                    else:
                        wait_bank(act, ("y_bank", 2 * g + (part == 2)), 3)
                for b in range(2):
                    act.activation(lm[:, 4 * b:4 * b + 4, :], X[:, b, :].rearrange("p (h l) -> p h l", h=4),
                                   ACT.Exp).then_inc(bank_free[b], 1)

            def gate_root(i):
                m = i % 2
                act.wait_ge(y_gated, i + 1)
                link(act.activation(xs[:, m, :], yy[:, m, :], ACT.Square, accum_out=ysq[:, m:m + 1]))
                act.activation(yrs[:, m:m + 1], ysq[:, m:m + 1], ACT.Sqrt, bias=eps[:], scale=1.0 / COLS)\
                   .then_inc(y_root, 1)

            def keep_y(g):
                for e in range(2):
                    wait_bank(act, ("turn_y", g), 2 + e)
                    for k in range(2):
                        kt = 4 * g + 2 * e + k
                        ins = act.activation(cT[:, 0, kt, :], X[:, 2 + e, k * SEQ:(k + 1) * SEQ], ACT.Copy,
                                             scale=par[:, G_SSD + kt:G_SSD + kt + 1])
                    ins.then_inc(yT_hi, 1)

            def sigmoid(b):
                kind, j = b
                act.wait_ge(chunk_used, end_of(b))
                if kind == "gs" or j:
                    wait_block(act, ACC[("att", 3 if kind == "gs" else j - 1)])
                for m in range(M):
                    act.activation(gate[:, m, :], acc[:, 2 * (ACC[b] % 2) + m, :], ACT.Sigmoid,
                                   scale=rstd[:, 0, m:m + 1]).then_inc(acc_free, 1)

            STEPS = dict(convert_consts=convert_consts, squares_x=squares_x, root_x=root_x, angles=angles,
                         keep_dt=keep_dt, keep_k=keep_k, keep_v=keep_v, keep_q=keep_q, exponents=exponents,
                         keep_p=keep_p, keep_o=keep_o, delta_exp=delta_exp, keep_sums=keep_sums,
                         sums_hi=sums_hi, keep_u=keep_u, last_tap=last_tap, silu=silu, keep_xs=keep_xs,
                         keep_z=keep_z, keep_cb=keep_cb, decay=decay, gate_root=gate_root, keep_y=keep_y,
                         sigmoid=sigmoid)

            act.wait_ge(par_in, 16)
            for h in range(2):
                split_transposed("x", aT, G_MIX, range(h * X_T // 2, (h + 1) * X_T // 2))
                for n in range(h * AHEAD // 2, (h + 1) * AHEAD // 2):
                    split(n)
            for n in range(AHEAD, N_LOOP_Y):
                split(n, size=KT * HEADS if n == START[("dt", 0)] else KPC * COLS)
                for name, arg in ACT_STEPS.get(n, []):
                    STEPS[name](arg)

            def keep_merged(turn, k_at):
                for e in range(2):
                    act.wait_ge(bank_full[e], turn + TURN[("merged", 0), e] + 1)
                    act.activation(bT[:, 0, k_at(2 * e), :], X[:, e, :].rearrange("p (k t) -> p k t", k=2),
                                   ACT.Copy).then_inc(merged_hi, 1)

            with act.Fori(0, LOOP_Y) as i:
                for c in range(2 * CPB):
                    split(N_LOOP_Y + c, 2 * CPB, i)
                    if c == CPB + 1:
                        keep_merged(i, lambda k: bass.ds(i * 4 + k, 2))
                    if c == CPB + 3:
                        act.wait_ge(chunk_used, N_LOOP_Y + CPB + i * 2 * CPB)
                        act.wait_ge(acc_free, i * 4 + 2 * BLK_LOOP_Y)
                        for m in range(M):
                            act.activation(gate[:, m, :], acc[:, 2 * (BLK_LOOP_Y % 2) + m, :], ACT.Sigmoid,
                                           scale=rstd[:, 0, m:m + 1]).then_inc(acc_free, 1)

            def square_projected(norm, blk, n_end, j):
                act.wait_ge(chunk_used, n_end)
                if norm > 2 or j:
                    act.wait_ge(block_sq, 8 * (norm // 2 - 1) + 2 * j)
                for m in range(M):
                    act.activation(gate[:, m, :], acc[:, 2 * (blk % 2) + m, :], ACT.Square,
                                   accum_out=ssq[:, norm, m, j:j + 1]).then_inc(block_sq, 1)

            def scaled_heads(dst, blk, n_end, norm):
                wait_norm(act, norm)
                act.wait_ge(chunk_used, n_end)
                for m in range(M):
                    act.activation(dst[:, m, :], acc[:, 2 * (blk % 2) + m, :], ACT.Copy,
                                   scale=rstd[:, norm, m:m + 1]).then_inc(acc_free, 1)

            for n in range(N_OUT, N_FFN):
                if n == N_XV + 3:
                    scaled_heads(xqk, BLK_XQ, N_XV, 3)
                if n == N_XO + 3:
                    scaled_heads(xv, BLK_XV, N_XO, 1)
                split(n)
                if n == N_OUT + 7:
                    keep_merged(LOOP_Y, lambda k: slice(LOOP_Y * 4 + k, LOOP_Y * 4 + k + 2))
                for j in range(4):
                    if n == N_OUT + (j + 1) * CPB + 3:
                        square_projected(2, BLK_OUT + j, n - 3, j)
                    if n == N_XO + (j + 1) * 2 + 3:
                        square_projected(4, BLK_XO + j, n - 3, j)
                if n in (N_OUT + 20, N_OUT + 21):
                    act.wait_ge(mem_in, 16)
                    squares(1, xm[:, n - N_OUT - 20, :], n - N_OUT - 20, junk[:])
                if n == N_OUT + 22:
                    root(1)
                if n in (N_OUT + 28, N_OUT + 31):
                    split_transposed("mem", aT, G_MEM, range(4) if n == N_OUT + 28 else range(4, X_T))
                if n == N_XK + 3:
                    root(2)
                if n in (N_XK + 6, N_XK + 7):
                    act.wait_ge(resid_ready, 4)
                    squares(3, xm[:, n - N_XK - 6, :], n - N_XK - 6, mix[:, n - N_XK - 6, :])
                if n == N_XK + 8:
                    split_transposed("h2", cT, G_XA, range(4))
                    root(3)
                if n == N_XK + 10:
                    split_transposed("h2", cT, G_XA, range(4, X_T))
                if n == N_XQ + 3:
                    scaled_heads(xqk, BLK_XK, N_XQ, 1)
                if n == N_XQ + 6:
                    for e in range(2):
                        keep(("xk", 0), e, xkT[:, 2 * e:2 * e + 2, :])
                if n == N_XV + 5:
                    keep(("xq", 0), 2, xqT[:, 0:2, :])
                if n == N_XV + 7:
                    for b in range(4):
                        act.wait_ge(xmax_ready, b + 1)
                        for h in range(2):
                            q = 2 * b + h
                            ins = act.activation(xp[:, b // 2, q % 4, :], X[:, b, h * SEQ:(h + 1) * SEQ], ACT.Exp,
                                                 bias=nmx[:, q:q + 1], scale=X_SCALE, accum_out=rsum[:, q:q + 1])
                        ins.then_inc(bank_free[b], 1)
                if n == N_XO + 2:
                    for e in range(2):
                        keep(("xturn_p0", 0), e, xpT[:, 0, 2 * e:2 * e + 2, :])
                if n == N_XO + 3:
                    for e in range(2):
                        wait_bank(act, ("xpv", 0), e)
                        act.activation(oT[:, 0, 2 * e:2 * e + 2, :], X[:, e, :].rearrange("p (k t) -> p k t", k=2),
                                       ACT.Copy).then_inc(xo_hi, 1)
            for n in range(N_FFN, N_FFN + AHEAD - 1):
                split(n)
                if n == N_FFN + 1:
                    square_projected(4, BLK_XO + 2, N_XO + 6, 2)
            square_projected(4, BLK_XO + 3, N_FFN, 3)
            root(4)
            split(N_FFN + AHEAD - 1)
            split_transposed("h3", aT, G_FFN)

            def silu_of(i, more):
                act.wait_ge(chunk_used, N_FFN + CPB + more * 2 * CPB)
                for m in range(M):
                    act.activation(hid[:, m, :], acc[:, 2 * (BLK_FFN % 2) + m, :], ACT.Silu,
                                   scale=rstd[:, 5, m:m + 1]).then_inc(acc_free, 1)

            def keep_hidden(i):
                act.wait_ge(bank_full[0], TURN[("hidden", 0), 0] + 1 + i)
                k_tiles = slice(4 * i, 4 * i + 2) if isinstance(i, int) else bass.ds(i * 4, 2)
                act.activation(hT[:, k_tiles, :], X[:, 0, :].rearrange("p (k t) -> p k t", k=2), ACT.Copy)\
                   .then_inc(bank_free[0], 1)

            for n in range(N_FFN + AHEAD, N_FFN + 2 * CPB):
                split(n)
                if n in (N_FFN + 5, N_FFN + 6):
                    act.wait_ge(resid_ready, 8)
                    squares(5, xm[:, n - N_FFN - 5, :], n - N_FFN - 5, mix[:, n - N_FFN - 5, :])
                if n == N_FFN + 7:
                    root(5)
                if n == N_FFN + CPB + 3:
                    wait_norm(act, 5)
                    silu_of(0, 0)
            with act.Fori(1, FBLOCKS) as i:
                for c in range(2 * CPB):
                    split(N_FFN + c, 2 * CPB, i)
                    if c == CPB + 2:
                        keep_hidden(i - 1)
                        act.wait_ge(bank_full[1], i + TURN[("hidden", 0), 1])
                    if c == CPB + 3:
                        silu_of(i, i)

            def split_hidden(i, k):
                if not (isinstance(i, int) and i == 0):
                    act.wait_ge(chunk_used, N_DOWN + DOWN_UNROLL + k + 1 + (i - 1) * 2 * DOWN_UNROLL)
                kt = bass.ds(i * DOWN_UNROLL + k, 1) if not isinstance(i, int) else slice(k, k + 1)
                act.activation(hq[:, k, 0:1, :], hT[:, kt, :], ACT.Copy).then_inc(hq_hi, 1)

            for k in range(DOWN_UNROLL):
                split_hidden(0, k)
            for c in range(2 * DOWN_UNROLL):
                split(N_DOWN + c)
                if c == DOWN_UNROLL:
                    keep_hidden(FBLOCKS - 1)
            for e in range(2):
                act.wait_ge(bank_free[e], TURN[("hidden", 0), e] + FBLOCKS)
            with act.Fori(1, DOWN_TURNS) as i:
                for k in range(DOWN_UNROLL):
                    split_hidden(i, k)
                    for c in (2 * k, 2 * k + 1):
                        split(N_DOWN + c, 2 * DOWN_UNROLL, i)
            for q in range(2):
                act.wait_ge(block_sq, 16 + 4 * q)
                for b in range(4):
                    act.wait_ge(down_done, 4 * q + b + 1)
                    j, m = 2 * q + (b // 2 + BLK_DOWN) % 2, b % 2
                    src = (acc if q == 0 else X)[:, 2 * (j % 2) + m, :]
                    act.activation(squared[:, b, :], src, ACT.Square, accum_out=ssq[:, 6, m, j:j + 1])\
                       .then_inc(block_sq, 1)
            root(6)

        @block.vector
        def _(dve):
            own = [0]

            def link(ins):
                own[0] += 1
                ins.then_inc(dve_step, 1)
                dve.wait_ge(dve_step, own[0])

            def f32(ap):
                return ap.bitcast(F32)

            def split(n, turns=0, i=0, size=KPC * COLS):
                dve.wait_ge(hi_ready, n + 1 + turns * i)
                s = n % SPLIT
                dve.tensor_tensor(lo[:, s, 0:size], raw[:, n % RAW, 0:size], f32(hi[:, s, 0:size]),
                                  ALU.subtract).then_inc(lo_ready, 1)

            def split_transposed(name, turn, dst, gain, turns=range(X_T)):
                for j in turns:
                    b = j % 4
                    dve.wait_ge(t_hi, turn * X_T + j + 1)
                    for k in range(2):
                        kt = 2 * j + k
                        ins = dve.scalar_tensor_tensor(out=dst[:, 1, kt, :], in0=X[:, b, k * SEQ:(k + 1) * SEQ],
                                                       scalar=par[:, gain + kt:gain + kt + 1],
                                                       in1=f32(dst[:, 0, kt, :]), op0=ALU.mult, op1=ALU.subtract)
                    ins.then_inc(bank_free[b], 1)

            def factor(norm):
                dve.wait_ge(root_ready, norm + 1)
                return dve.reciprocal(rstd[:, norm, :], rstd[:, norm, :])

            def sum_blocks(norm):
                dve.wait_ge(block_sq, 8 * (norm // 2))
                dve.tensor_reduce(rstd[:, norm, :], ssq[:, norm, :, :], AX.X, ALU.add).then_inc(sum_ready, 1)

            def rotate(blk, m, dsts):
                a = acc[:, 2 * (blk % 2) + m, :]
                sw = swapped[:].rearrange("p (h e r) -> p h e r", e=2, r=32)
                a4 = a.rearrange("p (h e r) -> p h e r", e=2, r=32)
                for e in range(2):
                    t = rope[:, 2 - e, m, :].unsqueeze(1).to_broadcast([P, 8, 32])
                    dve.tensor_tensor(sw[:, :, e, :], a4[:, :, 1 - e, :], t, ALU.mult)
                dve.tensor_tensor(qs[:, m, :].rearrange("p (h r) -> p h r", r=32),
                                  a.rearrange("p (h r) -> p h r", r=32),
                                  rope[:, 0, m, :].unsqueeze(1).to_broadcast([P, 16, 32]), ALU.mult)\
                   .then_inc(acc_free, 1)
                dve.wait_ge(acc_free, 2 * blk + m + 1)
                for dst in dsts:
                    ins = dve.tensor_tensor(dst, qs[:, m, :].rearrange("p (h d) -> p h d", d=HD),
                                            swapped[:].rearrange("p (h d) -> p h d", d=HD), ALU.add)
                return ins

            def rope_k(_):
                dve.wait_ge(chunk_used, end_of(("k", 0)))
                link(rotate(ACC[("k", 0)], 0, [kk[:, 0, :, e, :] for e in range(2)]))
                rotate(ACC[("k", 0)], 1, [kk[:, 1, :, e, :] for e in range(2)]).then_inc(k_roped, 1)

            def rope_q(b):
                dve.wait_ge(chunk_used, end_of(("q", b)))
                blk = ACC[("q", b)]
                link(rotate(blk, 0, [qs[:, 0, :].rearrange("p (h d) -> p h d", d=HD)]))
                rotate(blk, 1, [qs[:, 1, :].rearrange("p (h d) -> p h d", d=HD)]).then_inc(q_roped, 1)

            def maxima(u):
                h0 = 4 * u
                wait_bank(dve, ("scores", u), 0)
                dve.tensor_tensor(p0[:], X[:, 0, :].rearrange("p (h k) -> p h k", h=4),
                                  mask[:].unsqueeze(1).to_broadcast([P, 4, P]), ALU.add).then_inc(bank_free[0], 1)
                wait_bank(dve, ("scores", u), 1)
                dve.tensor_reduce(mx[:, 4:8], X[:, 1, :].rearrange("p (h k) -> p h k", h=4), AX.X, ALU.max)
                wait_kept(dve, ("scores", u), 0)
                link(dve.tensor_reduce(mx[:, 0:4], p0[:], AX.X, ALU.max))
                sink = row[:, R_SINK + h0:R_SINK + h0 + 4].unsqueeze(1).to_broadcast([P, 2, 4])
                mx2, esk2 = (t[:].rearrange("p (m h) -> p m h", m=M) for t in (mx, esk))
                link(dve.scalar_tensor_tensor(out=mx2, in0=mx2, scalar=ATT_SCALE, in1=sink, op0=ALU.mult,
                                              op1=ALU.max))
                dve.tensor_scalar(nmx[:], mx[:], -1.0, None, ALU.mult)
                dve.tensor_tensor(esk2, sink, mx2, ALU.subtract).then_inc(max_ready, 1)

            def probabilities(u):
                wait_kept(dve, ("scores", u), 1)
                link(dve.tensor_tensor(rsum[:], rsum[:], esk[:], ALU.add))
                link(dve.reciprocal(rsum[:], rsum[:]))
                for t, p in ((0, p0), (4, p1)):
                    ins = dve.tensor_tensor(p[:], p[:], rsum[:, t:t + 4].unsqueeze(2).to_broadcast([P, 4, P]),
                                            ALU.mult)
                ins.then_inc(probs_ready, 1)

            def keep_p(u):
                wait_bank(dve, ("turn_p", u), 1)
                dve.tensor_copy(pT[:, 1, :], X[:, 1, :]).then_inc(bank_free[1], 1)

            def keep_o(u):
                for m, b in enumerate(BANKS["pv"]):
                    o = X[:, b, :].rearrange("p (a e t) -> p a e t", a=2, e=2)
                    dve.wait_ge(o_hi, 4 * u + 2 * m + 2)
                    for e in range(2):
                        r = slice(HD * e, HD * e + HD)
                        t = slice(m * P, (m + 1) * P)
                        ins = dve.tensor_tensor(bT[r, 1, 2 * u:2 * u + 2, t], o[r, :, e, :],
                                                f32(bT[r, 0, 2 * u:2 * u + 2, t]), ALU.subtract)
                    ins.then_inc(bank_free[b], 1)

            def delta_in(_):
                t, a = sp[:, 0, :], sp[:, 1, :]
                wait_bank(dve, ("dt", 0), 3)
                for m in range(M):
                    h = slice(m * HEADS, (m + 1) * HEADS)
                    ins = dve.scalar_tensor_tensor(out=t[:, h], in0=X[:, 3, h], scalar=rstd[:, 0, m:m + 1],
                                                   in1=row[:, R_DTB:R_DTB + HEADS], op0=ALU.mult, op1=ALU.add)
                ins.then_inc(bank_free[3], 1)
                wait_kept(dve, ("dt", 0), 3)
                link(dve.tensor_scalar(a, t, -1.0, None, ALU.mult))
                dve.tensor_tensor(a, a, t, ALU.max).then_inc(sp_in, 1)

            def delta_series(_):
                u, z, z2, q = (sp[:, k, :] for k in range(2, 6))
                dve.wait_ge(sp_exp, 1)
                link(dve.tensor_scalar(z2, u, 2.0, None, ALU.add))
                link(dve.reciprocal(z2, z2))
                link(dve.tensor_tensor(z, u, z2, ALU.mult))
                link(dve.tensor_tensor(z2, z, z, ALU.mult))
                link(dve.tensor_scalar(q, z2, 1.0 / 15, None, ALU.mult))
                for k in (13, 11, 9, 7, 5, 3):
                    link(dve.scalar_tensor_tensor(out=q, in0=q, scalar=1.0 / k, in1=z2, op0=ALU.add, op1=ALU.mult))

            def delta_out(_):
                t, a, z, q = sp[:, 0, :], sp[:, 1, :], sp[:, 3, :], sp[:, 5, :]
                link(dve.scalar_tensor_tensor(out=q, in0=q, scalar=1.0, in1=z, op0=ALU.add, op1=ALU.mult))
                link(dve.tensor_scalar(a, t, 0.0, None, ALU.max))
                d = dt[:].rearrange("p m h -> p (m h)")
                link(dve.scalar_tensor_tensor(out=d, in0=q, scalar=2.0, in1=a, op0=ALU.mult, op1=ALU.add))
                for e in range(2):
                    ins = dve.scalar_tensor_tensor(
                        out=da2[:, :, e, :], in0=dt[:], scalar=-1.0,
                        in1=row[:, R_ALOG:R_ALOG + HEADS].unsqueeze(1).to_broadcast([P, M, HEADS]),
                        op0=ALU.mult, op1=ALU.mult)
                ins.then_inc(da_ready, 1)

            def keep_sums(_):
                wait_kept(dve, ("decay_sums", 0), 2)
                dve.tensor_scalar(csf[:, 2, :], csf[:, 0, :], csf[:, 0, P - 1:P], None, ALU.subtract)\
                   .then_inc(cse_ready, 1)

            def sums_lo(_):
                dve.wait_ge(chi_ready, 1)
                r = slice(HEADS, 2 * HEADS)
                dve.tensor_tensor(csq[r, :, :], csf[r, :, :], f32(chi[r, :, :]), ALU.subtract).then_inc(csq_lo, 1)

            def taps(i):
                t0 = 16 + 4 * i if i < 2 else 4 * (i - 2)
                for e, bank in enumerate(BANKS["turn_u"]):
                    dve.wait_ge(tap_ready, 4 * i + 2 * e + 2)
                    for s in (1, 2, 3):
                        for c in (2 * e, 2 * e + 1):
                            w = CONV_W + 24 * (3 - s) + t0 + c
                            o = uc[:, c * SEQ + s:(c + 1) * SEQ]
                            ins = dve.scalar_tensor_tensor(out=o, in0=X[:, bank, (c % 2) * SEQ:(c % 2 + 1) * SEQ - s],
                                                           scalar=par[:, w:w + 1], in1=o, op0=ALU.mult, op1=ALU.add)
                        if s < 3:
                            link(ins)
                        else:
                            ins.then_inc(bank_free[bank], 1)

            def keep_xs(g):
                for m, bank in enumerate(BANKS["turn_xs"]):
                    dve.wait_ge(xs_ready, 2 * g + m + 1)
                    dve.tensor_tensor(xdt[:, m, :].rearrange("p (h d) -> p h d", d=HD),
                                      X[:, bank, :].rearrange("p (h d) -> p h d", d=HD),
                                      dt[:, m, HPG * g:HPG * (g + 1)].unsqueeze(2).to_broadcast([P, HPG, HD]),
                                      ALU.mult).then_inc(bank_free[bank], 1)

            def decay(i):
                g, part = i // 3, i % 3
                if part == 0:
                    wait_kept(dve, ("cb", g), 2)
                for b in range(2):
                    wait_kept(dve, ("seg", i), b)
                c = cbs[:, part * P:(part + 1) * P].unsqueeze(1).to_broadcast([P, HPG, P])
                dve.tensor_tensor(lm[:], lm[:], c, ALU.mult).then_inc(m_ready, 1)

            def gate_y(i):
                g, m = i // 2, i % 2
                y, h3 = yy[:, m, :], (lambda ap: ap.rearrange("p (h d) -> p h d", d=HD))
                skip = row[:, R_DSKIP + HPG * g:R_DSKIP + HPG * (g + 1)].unsqueeze(2).to_broadcast([P, HPG, HD])
                link(dve.tensor_tensor(h3(y), h3(xs[:, m, :]), skip, ALU.mult))
                wait_bank(dve, ("y_bank", i), 3)
                dve.tensor_tensor(y, X[:, 3, :], y, ALU.add).then_inc(bank_free[3], 1)
                wait_kept(dve, ("y_bank", i), 3)
                wait_block(dve, ACC[("z", g)])
                dve.tensor_tensor(y, y, sz[:, m, :], ALU.mult).then_inc(y_gated, 1)

            def norm_y(i):
                m = i % 2
                y, r = yy[:, m, :], yrs[:, m:m + 1]
                dve.wait_ge(y_root, i + 1)
                link(dve.reciprocal(r, r))
                dve.tensor_scalar(y, y, r, None, ALU.mult).then_inc(y_normed, 1)

            def keep_y(g):
                for e in range(2):
                    dve.wait_ge(yT_hi, 2 * g + e + 1)
                    for k in range(2):
                        kt = 4 * g + 2 * e + k
                        ins = dve.scalar_tensor_tensor(out=cT[:, 1, kt, :], in0=X[:, 2 + e, k * SEQ:(k + 1) * SEQ],
                                                       scalar=par[:, G_SSD + kt:G_SSD + kt + 1],
                                                       in1=f32(cT[:, 0, kt, :]), op0=ALU.mult, op1=ALU.subtract)
                    ins.then_inc(bank_free[2 + e], 1)

            def merge_att(j):
                b = ("att", j)
                dve.wait_ge(chunk_used, end_of(b))
                wait_block(dve, ACC[b] - 1)
                for m in range(M):
                    dve.tensor_tensor(xm[:, m, j * COLS:(j + 1) * COLS], acc[:, 2 * (ACC[b] % 2) + m, :],
                                      gate[:, m, :], ALU.mult).then_inc(acc_free, 1)

            def angles(_):
                dve.wait_ge(pos_in, 16)
                dve.wait_ge(consts_in, 64)
                link(dve.tensor_copy(ysq[:], pos[:]))
                for m in range(M):
                    ins = dve.tensor_scalar(ang[:, 0, m * 32:(m + 1) * 32], ctmp[:, C_FREQ:C_FREQ + 32],
                                            ysq[:, m:m + 1], None, ALU.mult)
                link(ins)
                pi_a = 6.28125
                pi_b = float(np.float32(np.round((2 * np.pi - pi_a) * 2 ** 20) / 2 ** 20))
                pi_c = float(np.float32(2 * np.pi - pi_a - pi_b))
                for dst, quarter in ((4, 0.25), (5, 0.0)):
                    r, t = ang[:, dst, :], ang[:, 1, :]
                    link(dve.tensor_scalar(t, ang[:, 0, :], 1 / (2 * np.pi), quarter, ALU.mult, ALU.add))
                    link(dve.tensor_scalar(t, t, 12582912.0, None, ALU.add))
                    link(dve.tensor_scalar(t, t, -12582912.0, None, ALU.add))
                    link(dve.scalar_tensor_tensor(out=r, in0=t, scalar=-pi_a, in1=ang[:, 0, :], op0=ALU.mult,
                                                  op1=ALU.add))
                    for part in (pi_b, pi_c):
                        link(dve.scalar_tensor_tensor(out=r, in0=t, scalar=-part, in1=r, op0=ALU.mult, op1=ALU.add))
                    link(dve.tensor_scalar(r, r, quarter * 2 * np.pi, 3.1415925, ALU.add, ALU.min))
                    ins = dve.tensor_scalar(r, r, -3.1415925, None, ALU.max)
                    link(ins) if dst == 4 else ins.then_inc(angles_ready, 1)

            def norm_x(_):
                factor(0).then_inc(norm_ready, 1)
                wait_norm(dve, 0)
                dve.wait_ge(rope_ready, 1)
                link(dve.tensor_scalar(rope[:, 2, :, :], rope[:, 1, :, :], -1.0, None, ALU.mult))
                for m in range(M):
                    link(dve.tensor_scalar(rope[:, :, m, :], rope[:, :, m, :], rstd[:, 0, m:m + 1], None, ALU.mult))

            STEPS = dict(angles=angles, norm_x=norm_x, rope_k=rope_k, rope_q=rope_q, maxima=maxima,
                         probabilities=probabilities, keep_p=keep_p, keep_o=keep_o, delta_in=delta_in,
                         delta_series=delta_series, delta_out=delta_out, keep_sums=keep_sums, sums_lo=sums_lo,
                         taps=taps, keep_xs=keep_xs, decay=decay, gate_y=gate_y, norm_y=norm_y, keep_y=keep_y,
                         merge_att=merge_att)

            dve.wait_ge(par_in, 16)
            for h in range(2):
                split_transposed("x", 0, aT, G_MIX, range(h * X_T // 2, (h + 1) * X_T // 2))
                for n in range(h * AHEAD // 2, (h + 1) * AHEAD // 2):
                    split(n)
            for n in range(AHEAD, N_LOOP_Y):
                split(n, size=KT * HEADS if n == START[("dt", 0)] else KPC * COLS)
                for name, arg in DVE_STEPS.get(n, []):
                    STEPS[name](arg)

            def merge_y(turn, cols):
                blk, n_end = BLK_LOOP_Y - 1, N_LOOP_Y
                dve.wait_ge(chunk_used, n_end + turn * 2 * CPB)
                wait_block(dve, blk - 1, 4 * turn)
                for m in range(M):
                    dve.tensor_tensor(yy[:, m, :], acc[:, 2 * (blk % 2) + m, :], gate[:, m, :], ALU.mult)\
                       .then_inc(acc_free, 1)
                wait_block(dve, blk, 4 * turn)
                dve.tensor_tensor(yy[:, 0, :], yy[:, 0, :], xm[:, 0, cols], ALU.add)
                dve.tensor_tensor(yy[:, 1, :], yy[:, 1, :], xm[:, 1, cols], ALU.add).then_inc(merged_ready, 1)

            def keep_merged(turn, k_at):
                for e in range(2):
                    dve.wait_ge(merged_hi, 2 * turn + e + 1)
                    dve.tensor_tensor(bT[:, 1, k_at(2 * e), :], X[:, e, :].rearrange("p (k t) -> p k t", k=2),
                                      f32(bT[:, 0, k_at(2 * e), :]), ALU.subtract).then_inc(bank_free[e], 1)

            with dve.Fori(0, LOOP_Y) as i:
                for c in range(2 * CPB):
                    split(N_LOOP_Y + c, 2 * CPB, i)
                    if c == 3:
                        merge_y(i, bass.ds(i * COLS, COLS))
                    if c == CPB + 1:
                        keep_merged(i, lambda k: bass.ds(i * 4 + k, 2))

            def keep_projected(norm, blk, j, gain, tiles=range(M)):
                dve.wait_ge(gain_in, 16 * (norm // 2))
                for m in tiles:
                    dve.wait_ge(block_sq, 8 * (norm // 2 - 1) + 2 * j + m + 1)
                    dve.tensor_tensor(mix[:, m, j * COLS:(j + 1) * COLS], acc[:, 2 * (blk % 2) + m, :],
                                      gain[:, j * COLS:(j + 1) * COLS], ALU.mult).then_inc(acc_free, 1)

            def add_residual(norm, q, residual):
                cols = slice(q * COLS, (q + 1) * COLS)
                for m in range(M):
                    ins = dve.scalar_tensor_tensor(out=xm[:, m, cols], in0=mix[:, m, cols],
                                                   scalar=rstd[:, norm, m:m + 1], in1=residual[:, m, cols],
                                                   op0=ALU.mult, op1=ALU.add)
                ins.then_inc(resid_ready, 1)

            for n in range(N_OUT, N_FFN):
                split(n)
                if n == N_OUT + 3:
                    merge_y(LOOP_Y, slice(LOOP_Y * COLS, (LOOP_Y + 1) * COLS))
                if n == N_OUT + 7:
                    keep_merged(LOOP_Y, lambda k: slice(LOOP_Y * 4 + k, LOOP_Y * 4 + k + 2))
                for j in range(4):
                    if n == N_OUT + (j + 1) * CPB + 3:
                        keep_projected(2, BLK_OUT + j, j, gb)
                    if n == N_XO + (j + 1) * 2 + 3:
                        keep_projected(4, BLK_XO + j, j, gx)
                if n == N_OUT + 23:
                    factor(1).then_inc(norm_ready, 1)
                if n in (N_OUT + 28, N_OUT + 31):
                    split_transposed("mem", 1, aT, G_MEM, range(4) if n == N_OUT + 28 else range(4, X_T))
                if n == N_XK + 3:
                    sum_blocks(2)
                    dve.wait_ge(bank_full[3], TURN[("mem", X_T - 1), 3] + 1)
                    dve.wait_ge(x_again, 16)
                if n == N_XK + 4:
                    link(factor(2))
                    wait_block(dve, BLK_OUT + 3)
                    add_residual(2, 0, xr)
                    add_residual(2, 1, xr)
                if n == N_XK + 5:
                    add_residual(2, 2, xr)
                    add_residual(2, 3, xr)
                if n == N_XK + 8:
                    split_transposed("h2", 2, cT, G_XA, range(4))
                if n == N_XK + 9:
                    factor(3).then_inc(norm_ready, 1)
                if n == N_XK + 10:
                    split_transposed("h2", 2, cT, G_XA, range(4, X_T))
                if n == N_XV + 5:
                    wait_bank(dve, ("xq", 0), 3)
                    dve.tensor_copy(xqT[:, 2:4, :], X[:, 3, :].rearrange("p (k t) -> p k t", k=2))\
                       .then_inc(bank_free[3], 1)
                if n == N_XV + 7:
                    for b in range(4):
                        wait_bank(dve, ("xscores", 0), b)
                        link(dve.tensor_reduce(mx[:, 2 * b:2 * b + 2],
                                               X[:, b, :].rearrange("p (h k) -> p h k", h=2), AX.X, ALU.max))
                        dve.tensor_scalar(nmx[:, 2 * b:2 * b + 2], mx[:, 2 * b:2 * b + 2], -X_SCALE, None,
                                          ALU.mult).then_inc(xmax_ready, 1)
                if n == N_XO:
                    for b in range(4):
                        wait_kept(dve, ("xscores", 0), b)
                    link(dve.reciprocal(rsum[:], rsum[:]))
                    for m in range(M):
                        dve.tensor_tensor(xp[:, m, :, :], xp[:, m, :, :],
                                          rsum[:, 4 * m:4 * m + 4].unsqueeze(2).to_broadcast([P, XH, SEQ]),
                                          ALU.mult).then_inc(xp_ready, 1)
                if n == N_XO + 2:
                    for e in range(2):
                        wait_bank(dve, ("xturn_p1", 0), 2 + e)
                        dve.tensor_copy(xpT[:, 1, 2 * e:2 * e + 2, :],
                                        X[:, 2 + e, :].rearrange("p (k t) -> p k t", k=2))\
                           .then_inc(bank_free[2 + e], 1)
                if n == N_XO + 3:
                    for e in range(2):
                        dve.wait_ge(xo_hi, e + 1)
                        dve.tensor_tensor(oT[:, 1, 2 * e:2 * e + 2, :],
                                          X[:, e, :].rearrange("p (k t) -> p k t", k=2),
                                          f32(oT[:, 0, 2 * e:2 * e + 2, :]), ALU.subtract)\
                           .then_inc(bank_free[e], 1)
            for n in range(N_FFN, N_FFN + AHEAD - 1):
                split(n)
                if n == N_FFN + 1:
                    keep_projected(4, BLK_XO + 2, 2, gx)
            keep_projected(4, BLK_XO + 3, 3, gx, [0])
            sum_blocks(4)
            keep_projected(4, BLK_XO + 3, 3, gx, [1])
            link(factor(4))
            wait_block(dve, BLK_XO + 3)
            add_residual(4, 0, xm)
            for q in range(1, 4):
                add_residual(4, q, xm)
                split_transposed("h3", 3, aT, G_FFN, range(2 * q - 2, 2 * q))
                if q == 1:
                    split(N_FFN + AHEAD - 1)
            split_transposed("h3", 3, aT, G_FFN, range(6, X_T))

            def hidden(pair):
                blk = BLK_FFN + 1
                dve.wait_ge(chunk_used, N_FFN + 2 * CPB + pair * 2 * CPB)
                wait_block(dve, blk - 1, 4 * pair)
                for m in range(M):
                    dve.scalar_tensor_tensor(out=hid[:, m, :], in0=acc[:, 2 * (blk % 2) + m, :],
                                             scalar=rstd[:, 5, m:m + 1], in1=hid[:, m, :], op0=ALU.mult,
                                             op1=ALU.mult).then_inc(acc_free, 1)

            def keep_hidden(i):
                dve.wait_ge(bank_full[1], TURN[("hidden", 0), 1] + 1 + i)
                k_tiles = slice(4 * i + 2, 4 * i + 4) if isinstance(i, int) else bass.ds(i * 4 + 2, 2)
                dve.tensor_copy(hT[:, k_tiles, :], X[:, 1, :].rearrange("p (k t) -> p k t", k=2))\
                   .then_inc(bank_free[1], 1)

            for n in range(N_FFN + AHEAD, N_FFN + 2 * CPB):
                split(n)
                if n == N_FFN + CPB:
                    factor(5).then_inc(norm_ready, 1)
                    wait_norm(dve, 5)
            with dve.Fori(1, FBLOCKS) as i:
                for c in range(2 * CPB):
                    split(N_FFN + c, 2 * CPB, i)
                    if c == 3:
                        hidden(i - 1)
                    if c == CPB + 2:
                        keep_hidden(i - 1)

            def split_hidden(i, k):
                dve.wait_ge(hq_hi, i * DOWN_UNROLL + k + 1)
                kt = bass.ds(i * DOWN_UNROLL + k, 1) if not isinstance(i, int) else slice(k, k + 1)
                dve.tensor_tensor(hq[:, k, 1:2, :], hT[:, kt, :], f32(hq[:, k, 0:1, :]), ALU.subtract)\
                   .then_inc(hq_lo, 1)

            for k in range(DOWN_UNROLL):
                split_hidden(0, k)
            for c in range(2 * DOWN_UNROLL):
                if c == AHEAD - 1:
                    hidden(FBLOCKS - 1)
                split(N_DOWN + c)
                if c == DOWN_UNROLL:
                    keep_hidden(FBLOCKS - 1)
            with dve.Fori(1, DOWN_TURNS) as i:
                for k in range(DOWN_UNROLL):
                    split_hidden(i, k)
                    for c in (2 * k, 2 * k + 1):
                        split(N_DOWN + c, 2 * DOWN_UNROLL, i)
            dve.wait_ge(gain_in, 48)
            for q in range(2 * M * 2):
                j, m = 2 * (q // 4) + (q % 4 // 2 + BLK_DOWN) % 2, q % 2
                cols = slice(j * COLS, (j + 1) * COLS)
                dve.wait_ge(block_sq, 16 + q + 1)
                ins = dve.tensor_tensor(projected[:, m, cols], (acc if j < 2 else X)[:, 2 * (j % 2) + m, :],
                                        gf[:, cols], ALU.mult)
            link(ins)
            sum_blocks(6)
            link(factor(6))
            for m in range(M):
                for j in range(4):
                    cols = slice(j * COLS, (j + 1) * COLS)
                    dve.scalar_tensor_tensor(out=xm[:, m, cols], in0=projected[:, m, cols],
                                             scalar=rstd[:, 6, m:m + 1], in1=xm[:, m, cols], op0=ALU.mult,
                                             op1=ALU.add).then_inc(out_ready, 1)


BIG = ["x", "mem", "positions", "w_in", "w_attn_branch", "w_ssd_branch", "w_out", "xa_wq", "xa_wk", "xa_wv",
       "xa_wo", "ffn_wg", "ffn_wu", "ffn_wd"]


def constants():
    c = np.zeros((P, C_TOTAL), np.float32)
    r = np.arange(P)
    c[:, C_IDENT:C_IDENT + P] = np.eye(P)
    c[:, C_TRI:C_TRI + P] = r[:, None] <= r[None, :]
    chunk = r[:, None] // 64
    c[:, C_MASK:C_MASK + P] = np.where(r[None, :] // 64 <= chunk, 0, NEG)
    c[:, C_CNEG:C_CNEG + P] = np.where(r[:, None] <= r[None, :], 0, NEG)
    c[:, C_FREQ:C_FREQ + 32] = np.float32(10000.0) ** (-np.arange(0, HD, 2, dtype=np.float32) / np.float32(HD))
    c[:, C_SEL:C_SEL + HEADS] = r[:, None] % HEADS == np.arange(HEADS)[None, :]
    c[:, C_EPS] = EPS
    return c


def kernel(**inputs):
    import concourse.bacc as bacc
    from concourse.bass_utils import run_bass_kernel_spmd

    nc = bacc.Bacc("TRN2", target_bir_lowering=False, num_devices=1)
    given = {k: np.asarray(v) for k, v in inputs.items()}
    arrays = {}
    for name in BIG:
        a = given[name]
        arrays[name] = np.ascontiguousarray(a if name in ("x", "mem", "positions") else a[0])
    arrays["positions"] = np.ascontiguousarray(given["positions"].reshape(M, P).T)

    def columns(a):
        return np.ascontiguousarray(a.reshape(-1, P).T)

    arrays["params"] = np.concatenate([columns(given[k]) for k in (
        "mix_pre_g", "xa_pre_g", "xa_mem_g", "ffn_pre_g", "ssd_norm_g", "conv_b", "conv_w")], axis=1)
    arrays["rows"] = np.concatenate([given[k] for k in ("dt_bias", "a_log", "d_skip", "attn_sink")], axis=1)
    arrays["post_gains"] = np.concatenate([given[k] for k in ("mix_post_g", "xa_post_g", "ffn_post_g")], axis=0)
    arrays["consts"] = constants()
    args = [nc.dram_tensor(f"in_{k}", a.shape, mybir.dt.from_np(a.dtype), kind="ExternalInput").ap()
            for k, a in arrays.items()]
    out = nc.dram_tensor("out", given["x"].shape, F32, kind="ExternalOutput").ap()
    trunk(nc, *args, out)
    r = run_bass_kernel_spmd(nc, [{f"in_{k}": a for k, a in arrays.items()}], core_ids=[0])
    return r.results[0]["out"]
```
